# Optimizing a Trainium2 kernel written in Bass

```python
import jax, jax.numpy as jnp
from jax import lax
import numpy as np

D_MODEL = 1024
BATCH = 1
SEQ = 512
DEPTH = 2

HEAD_DIM = 64
GRID_W = 64
NA_HEADS = 4
NA_WIN_ROWS = 8
NA_WIN_COLS = 16
DIL_HEADS = 6
DIL_PATTERNS = ((128, 1), (512, 4), (2048, 16))
DIL_Q_BLOCK = 128
CONV_CH = 384
CONV_WIDTH = 31
ROPE_THETA = 10000.0
NORM_EPS = 1e-6
NEG_INF = -1e30
NA_W = NA_HEADS * HEAD_DIM
DIL_W = DIL_HEADS * HEAD_DIM
D_MIX = NA_W + DIL_W + CONV_CH
D_IN = 4 * NA_W + 4 * DIL_W + 3 * CONV_CH

kernel_name = "hybrid_na_dilated_conformer_block"

def rms_norm(x, g):
    xf = x.astype(jnp.float32)
    y = xf * lax.rsqrt(jnp.mean(xf * xf, axis=-1, keepdims=True) + NORM_EPS)
    return (y * g.astype(jnp.float32)).astype(x.dtype)

def rotary(x, pos):
    half = HEAD_DIM // 2
    inv_freq = jnp.power(ROPE_THETA, -jnp.arange(half, dtype=jnp.float32) * 2.0 / HEAD_DIM)
    ang = pos.astype(jnp.float32)[:, None] * inv_freq[None, :]
    cos = jnp.cos(ang)[None, :, None, :]
    sin = jnp.sin(ang)[None, :, None, :]
    xf = x.astype(jnp.float32)
    x1, x2 = xf[..., :half], xf[..., half:]
    return jnp.concatenate([x1 * cos - x2 * sin, x2 * cos + x1 * sin], axis=-1).astype(x.dtype)

def neighbourhood_attention(q, k, v, rpb):
    B, S, H, dh = q.shape
    rows = S // GRID_W
    kh = min(NA_WIN_ROWS, rows)
    kw = NA_WIN_COLS

    def to_grid(t):
        return t.reshape(B, rows, GRID_W, H, dh).transpose(1, 0, 3, 2, 4)

    qg, kg, vg = to_grid(q), to_grid(k), to_grid(v)
    cols = np.arange(GRID_W)
    col_start = np.clip(cols - kw // 2, 0, GRID_W - kw)
    col_idx = col_start[:, None] + np.arange(kw)[None, :]
    col_off = col_idx - cols[:, None] + (NA_WIN_COLS - 1)
    bias_cols = rpb[:, :, col_off]
    scale = HEAD_DIM ** -0.5

    def row_step(args):
        q_row, r = args
        r0 = jnp.clip(r - kh // 2, 0, rows - kh)
        k_rows = lax.dynamic_slice_in_dim(kg, r0, kh, axis=0)
        v_rows = lax.dynamic_slice_in_dim(vg, r0, kh, axis=0)
        k_win = k_rows[:, :, :, col_idx]
        v_win = v_rows[:, :, :, col_idx]
        row_off = r0 + jnp.arange(kh) - r + (NA_WIN_ROWS - 1)
        bias = bias_cols[:, row_off].transpose(0, 2, 1, 3)
        s = jnp.einsum('bhcd,ibhcjd->bhcij', q_row, k_win).astype(jnp.float32) * scale
        s = s + bias[None].astype(jnp.float32)
        p = jax.nn.softmax(s.reshape(B, H, GRID_W, kh * kw), axis=-1)
        p = p.reshape(B, H, GRID_W, kh, kw).astype(v.dtype)
        return jnp.einsum('bhcij,ibhcjd->bhcd', p, v_win)

    out = lax.map(row_step, (qg, jnp.arange(rows)))
    return out.transpose(1, 0, 3, 2, 4).reshape(B, S, H * dh)

def dilated_attention(q, k, v):
    B, S, H, dh = q.shape
    nblk = S // DIL_Q_BLOCK
    kt = k.transpose(0, 2, 1, 3)
    vt = v.transpose(0, 2, 1, 3)
    qb = q.transpose(0, 2, 1, 3).reshape(B, H, nblk, DIL_Q_BLOCK, dh).transpose(2, 0, 1, 3, 4)
    offsets = [d * np.arange(-((w // 2) // d), (w // 2) // d + 1) for (w, d) in DIL_PATTERNS]
    scale = HEAD_DIM ** -0.5

    def block_step(args):
        q_blk, start = args
        pos = start + jnp.arange(DIL_Q_BLOCK)
        outs, lses = [], []
        for off in offsets:
            idx = pos[:, None] + off[None, :]
            valid = (idx >= 0) & (idx < S)
            idx_c = jnp.clip(idx, 0, S - 1)
            k_sel = jnp.take(kt, idx_c, axis=2)
            v_sel = jnp.take(vt, idx_c, axis=2)
            s = jnp.einsum('bhqd,bhqnd->bhqn', q_blk, k_sel).astype(jnp.float32) * scale
            s = jnp.where(valid, s, NEG_INF)
            lse = jax.nn.logsumexp(s, axis=-1, keepdims=True)
            p = jnp.exp(s - lse).astype(v.dtype)
            outs.append(jnp.einsum('bhqn,bhqnd->bhqd', p, v_sel).astype(jnp.float32))
            lses.append(lse)
        wts = jax.nn.softmax(jnp.stack(lses, axis=0), axis=0)
        return jnp.sum(wts * jnp.stack(outs, axis=0), axis=0).astype(q.dtype)

    out = lax.map(block_step, (qb, jnp.arange(nblk) * DIL_Q_BLOCK))
    return out.transpose(1, 0, 3, 2, 4).reshape(B, S, H * dh)

def conformer_conv(a, b, w_dw, b_dw, ln_g, ln_b, w_pw, b_pw):
    u = a * jax.nn.sigmoid(b)
    y = lax.conv_general_dilated(
        u, w_dw[:, None, :].astype(u.dtype), window_strides=(1,),
        padding=[(CONV_WIDTH // 2, CONV_WIDTH // 2)],
        dimension_numbers=('NWC', 'WIO', 'NWC'), feature_group_count=CONV_CH) + b_dw
    yf = y.astype(jnp.float32)
    mu = jnp.mean(yf, axis=-1, keepdims=True)
    var = jnp.mean(jnp.square(yf - mu), axis=-1, keepdims=True)
    yn = ((yf - mu) * lax.rsqrt(var + NORM_EPS) * ln_g.astype(jnp.float32) + ln_b.astype(jnp.float32)).astype(u.dtype)
    return jax.nn.silu(yn) @ w_pw + b_pw

def hybrid_layer(x, g, w_in, rpb, w_dw, b_dw, ln_g, ln_b, w_pw, b_pw, w_out, pos):
    B, S, _ = x.shape
    h = rms_norm(x, g)
    z = h @ w_in
    splits = [int(s) for s in np.cumsum([NA_W] * 4 + [DIL_W] * 4 + [CONV_CH] * 2)]
    aq, ak, av, ag, bq, bk, bv, bg, ca, cb, cg = jnp.split(z, splits, axis=-1)

    def heads(t, n):
        return t.reshape(B, S, n, HEAD_DIM)

    ya = neighbourhood_attention(heads(aq, NA_HEADS), heads(ak, NA_HEADS), heads(av, NA_HEADS), rpb)
    ya = ya * jax.nn.silu(ag)
    yb = dilated_attention(rotary(heads(bq, DIL_HEADS), pos), rotary(heads(bk, DIL_HEADS), pos),
                           heads(bv, DIL_HEADS))
    yb = yb * jax.nn.silu(bg)
    yc = conformer_conv(ca, cb, w_dw, b_dw, ln_g, ln_b, w_pw, b_pw) * jax.nn.silu(cg)
    return x + jnp.concatenate([ya, yb, yc], axis=-1) @ w_out

def setup_inputs(seed: int = 0) -> dict:
    key = jax.random.key(seed)
    ks = jax.random.split(key, 13)
    f32 = jnp.float32
    x = jax.random.normal(ks[0], (BATCH, SEQ, D_MODEL), f32)
    norm_g = 1.0 + 0.01 * jax.random.normal(ks[1], (DEPTH, D_MODEL), f32)
    w_in = jax.random.normal(ks[2], (DEPTH, D_MODEL, D_IN), f32) * D_MODEL ** -0.5
    na_rpb = 0.02 * jax.random.normal(ks[3], (DEPTH, NA_HEADS, 2 * NA_WIN_ROWS - 1, 2 * NA_WIN_COLS - 1), f32)
    conv_w = jax.random.normal(ks[4], (DEPTH, CONV_WIDTH, CONV_CH), f32) * CONV_WIDTH ** -0.5
    conv_b = 0.01 * jax.random.normal(ks[5], (DEPTH, CONV_CH), f32)
    conv_ln_g = 1.0 + 0.01 * jax.random.normal(ks[6], (DEPTH, CONV_CH), f32)
    conv_ln_b = 0.01 * jax.random.normal(ks[7], (DEPTH, CONV_CH), f32)
    pw_w = jax.random.normal(ks[8], (DEPTH, CONV_CH, CONV_CH), f32) * CONV_CH ** -0.5
    pw_b = 0.01 * jax.random.normal(ks[9], (DEPTH, CONV_CH), f32)
    w_out = jax.random.normal(ks[10], (DEPTH, D_MIX, D_MODEL), f32) * D_MIX ** -0.5
    final_g = 1.0 + 0.01 * jax.random.normal(ks[11], (D_MODEL,), f32)
    return {"x": x, "norm_g": norm_g, "w_in": w_in, "na_rpb": na_rpb, "conv_w": conv_w,
            "conv_b": conv_b, "conv_ln_g": conv_ln_g, "conv_ln_b": conv_ln_b, "pw_w": pw_w,
            "pw_b": pw_b, "w_out": w_out, "final_g": final_g}

def reference(x, norm_g, w_in, na_rpb, conv_w, conv_b, conv_ln_g, conv_ln_b, pw_w, pw_b, w_out, final_g):
    pos = jnp.arange(x.shape[1])
    h = x
    for l in range(DEPTH):
        h = hybrid_layer(h, norm_g[l], w_in[l], na_rpb[l], conv_w[l], conv_b[l], conv_ln_g[l],
                         conv_ln_b[l], pw_w[l], pw_b[l], w_out[l], pos)
    return rms_norm(h, final_g)


_drawn_inputs = setup_inputs


def setup_inputs(seed=0):
    import zlib

    import numpy as np

    out = dict(_drawn_inputs(seed))
    spreads = {}
    factors = {'norm_g': 8.0,
     'na_rpb': 8.0,
     'conv_b': 8.0,
     'conv_ln_g': 8.0,
     'conv_ln_b': 8.0,
     'pw_b': 8.0,
     'final_g': 5.652}
    for name, (base, spread) in spreads.items():
        noise = np.random.default_rng([zlib.crc32(name.encode()), seed]).standard_normal(out[name].shape)
        drawn = base * np.exp(spread * noise) if base else spread * noise
        out[name] = __import__('jax').numpy.asarray(drawn.astype(out[name].dtype))
    for name, factor in factors.items():
        out[name] = (out[name] * factor).astype(out[name].dtype)
    return out
```

```python
from contextlib import ExitStack

import numpy as np
import concourse.bass as bass
from concourse import mybir

F32 = mybir.dt.float32
F32R = mybir.dt.float32r
ALU = mybir.AluOpType
ACT = mybir.ActivationFunctionType

P = 128
SEQ = 512
D = 1024
DEPTH = 2
GRID_W = 64
ROWS = SEQ // GRID_W
HD = 64
NA_HEADS, DIL_HEADS = 4, 6
WIN_COLS = 16
PATTERNS = ((128, 1), (512, 4), (2048, 16))
CONV_CH = 384
TAPS = 31
HALO = TAPS // 2
EPS = 1e-6
NEG = -1e30
KD = D // P
CT = CONV_CH // P
QT = SEQ // P

IN_TILES = [("cb", 0), ("ca", 0), ("cb", 1), ("ca", 1), ("cb", 2), ("ca", 2),
            ("bq", 0), ("bk", 0), ("bv", 0),
            ("bq", 1), ("bk", 1), ("bv", 1), ("bg", 0),
            ("bq", 2), ("bk", 2), ("bv", 2), ("bg", 1),
            ("aq", 0), ("ak", 0), ("av", 0), ("bg", 2),
            ("aq", 1), ("ak", 1), ("av", 1), ("ag", 0),
            ("ag", 1), ("cg", 0), ("cg", 1), ("cg", 2)]
PART_AT = {"aq": 0, "ak": 256, "av": 512, "ag": 768, "bq": 1024, "bk": 1408, "bv": 1792, "bg": 2176,
           "ca": 2560, "cb": 2944, "cg": 3328}
N_IN = len(IN_TILES)
PRE = 9
N_CH = N_IN + CT + KD
RAW = 4
SPL = 4
AHEAD = SPL - 1
LOAD_AHEAD = AHEAD + RAW
assert N_CH % RAW == 0 and N_CH % SPL == 0

PAIRS = 5
DPAIRS = DIL_HEADS // 2
UPP = 8
UNITS = PAIRS * UPP
DUNITS = DPAIRS * UPP
Y_OF_PAIR = [2, 3, 4, 0, 1]
K_ORDER = [2, 3, 4, 0, 5, 6, 7, 1]
NAW = 32
NA_LO = [0, 8, 24, 32]
NKEY = ROWS * NAW
NEG_TILE = 896
PREP = 8 + CT * TAPS + 4 * CT
P_G, P_W, P_B = 0, 8, 8 + CT * TAPS
P_LG, P_LB, P_PB = P_B + CT, P_B + 2 * CT, P_B + 3 * CT

LN_MEAN, LN_COL, LN_BC, LN_SILU = 27, 29, 30, 32
PRE_TAPS, SLOT_TAPS = 7, 2


def unit(n):
    return n // UPP, n % 2, (n % UPP) // 2


def build(nc, xT, w_in, w_pw, w_out, prm, gfin, nabias, lncnt, rope, out):
    with ExitStack() as ctx:
        def sb(name, shape, dt=F32):
            return ctx.enter_context(nc.sbuf_tensor(name, shape, dt))

        def bank(name):
            return ctx.enter_context(nc.psum_tensor(name, [P, SEQ], F32))

        def sem(name):
            return ctx.enter_context(nc.semaphore(name))

        x = sb("x", [P, KD, SEQ])
        act_hi = sb("act_hi", [P, KD, SEQ], F32R)
        act_lo = sb("act_lo", [P, KD, SEQ], F32R)
        y = sb("y", [P, KD, SEQ])
        raw = sb("raw", [P, RAW, KD, P])
        w_hi = sb("w_hi", [P, SPL, KD, P], F32R)
        w_lo = sb("w_lo", [P, SPL, KD, P], F32R)
        qpad = sb("qpad", [P, 2, 2, SEQ])
        kT = sb("kT", [P, 2, SEQ])
        v = sb("v", [P, 2, 2 * QT, P])
        vT = sb("vT", [P, SEQ])
        zs = sb("zs", [P, SEQ])
        zsw = sb("zsw", [P, SEQ])
        zc = sb("zc", [P, SEQ])
        u = sb("u", [P, CT, SEQ + 2 * HALO])
        acc2 = sb("acc2", [P, SEQ])
        s_hi = sb("s_hi", [P, CT, SEQ], F32R)
        s_lo = sb("s_lo", [P, CT, SEQ], F32R)
        th = sb("th", [P, SEQ])
        prob = sb("prob", [P, 3, SEQ])
        pT = sb("pT", [P, 2, QT, SEQ])
        bias = sb("bias", [P, 2, NKEY])
        sq = sb("sq", [P, 2, SEQ])
        ssq = sb("ssq", [P, SEQ])
        rstd = sb("rstd", [P, SEQ])
        diag = sb("diag", [P, QT, P])
        cnt = sb("cnt", [P, NEG_TILE])
        cs = sb("cs", [P, 2, SEQ])
        ident = sb("ident", [P, P])
        ones = sb("ones", [P, P])
        mean_w = sb("mean_w", [P, P])
        par = sb("par", [P, PREP])
        parh = sb("parh", [P, 2 * CT])
        gf = sb("gf", [P, KD])
        nmx = sb("nmx", [P, 4])
        den = sb("den", [P, 4])
        rden = sb("rden", [P, 4])
        col = sb("col", [P, QT])
        rcol = sb("rcol", [P, QT])
        nhalf = sb("nhalf", [P, QT])

        acc = [bank("acc0"), bank("acc1")]
        sc = [bank("sc0"), bank("sc1")]
        tp = [bank("tp0"), bank("tp1")]
        ob = bank("ob")
        misc = bank("misc")

        raw_in = [sem(f"raw_in{i}") for i in range(RAW)]
        x_in = sem("x_in")
        const_in = sem("const_in")
        par_in = sem("par_in")
        bias_in = [sem(f"bias_in{i}") for i in range(2)]
        swap_in = sem("swap_in")
        out_in = sem("out_in")
        consts = sem("consts")
        cleared = sem("cleared")
        hi_ready = sem("hi_ready")
        lo_ready = sem("lo_ready")
        xhi_ready = sem("xhi_ready")
        xlo_ready = sem("xlo_ready")
        yhi_ready = sem("yhi_ready")
        ylo_ready = sem("ylo_ready")
        tile_done = sem("tile_done")
        acc_free = sem("acc_free")
        sq_ready = sem("sq_ready")
        add_done = sem("add_done")
        misc_ready = sem("misc_ready")
        misc_free = sem("misc_free")
        pow_ready = sem("pow_ready")
        diag_ready = sem("diag_ready")
        cbt_ready = sem("cbt_ready")
        u_ready = sem("u_ready")
        conv_step = sem("conv_step")
        t2_ready = sem("t2_ready")
        qk_ready = sem("qk_ready")
        s_ready = sem("s_ready")
        m_ready = sem("m_ready")
        e_ready = sem("e_ready")
        r_ready = sem("r_ready")
        p_ready = sem("p_ready")
        t_ready = sem("t_ready")
        pt_ready = sem("pt_ready")
        pv_done = sem("pv_done")
        pair_final = sem("pair_final")
        th_ready = sem("th_ready")
        th_used = sem("th_used")
        hn_ready = sem("hn_ready")
        shi_ready = sem("shi_ready")
        slo_ready = sem("slo_ready")
        dve_own = sem("dve_own")
        res_ready = sem("res_ready")

        MISC_COL, MISC_BC = 0, 1
        MISC_V = {0: [2], 1: [3], 2: [4], 3: [5, 6], 4: [10, 11]}
        MISC_MEAN, MISC_LCOL, MISC_LBC = 7, 8, 9
        MISC_L = 12
        V_AT = {1: [(0, 0)]} | {UPP * g - 1 + rnd: [(g, rnd)] for g in range(1, PAIRS) for rnd in range(len(MISC_V[g]))}
        ROPES = 2 * DPAIRS
        ADD_L = (KD - 1) + (CT - 1)
        SQ_L = KD + CT
        STEPS = CT * (TAPS + 1)
        ACC0 = N_CH + 2

        def chunk_src(l, c):
            if c < N_IN:
                return w_in[l, c], KD
            if c < N_IN + CT:
                return w_pw[l, c - N_IN], CT
            return w_out[l, c - N_IN - CT], KD

        def rows_of(c):
            return CT if N_IN <= c < N_IN + CT else KD

        def follows(l, c):
            l, c = (l, c) if c < N_CH else (l + 1, c - N_CH)
            return (l, c) if l < DEPTH else None

        TH_SEQ = [("bg", 0), ("bg", 1), ("bg", 2), ("ln", 0), ("ag", 0), ("ln", 1), ("ln", 2), ("ag", 1),
                  ("cg", 0), ("cg", 1), ("cg", 2)]
        TH_L = len(TH_SEQ)
        Y_OF_GATE = {"ag": 0, "bg": 2, "cg": 5}

        def emptied(l, c):
            return ACC0 + N_CH * l + c + 1

        def x_tile(l, k):
            return emptied(l - 1, N_IN + CT + k)

        def v_tile(g):
            return IN_TILES.index(("bv", g) if g < DPAIRS else ("av", g - DPAIRS))

        def rope_of(c):
            kind, j = IN_TILES[c]
            return 2 * j + (kind == "bk") if kind in ("bq", "bk") else None

        def tile_at(n):
            return PRE + n // 2, n % 2 == 1

        block = ctx.enter_context(nc.Block())

        @block.sync
        def _(sp):
            def load(l, c, wait):
                src, k = chunk_src(l, c)
                if wait:
                    sp.wait_ge(lo_ready, N_CH * l + c - RAW + 1)
                sp.dma_start(raw[:, c % RAW, 0:k, :], src).then_inc(raw_in[c % RAW], 16)

            def load_next(l, c):
                if (f := follows(l, c + LOAD_AHEAD)) is not None:
                    load(*f, True)

            def swap(l, r):
                sp.wait_ge(acc_free, emptied(l, IN_TILES.index(("bk" if r % 2 else "bq", r // 2))))
                for h in range(4):
                    o = 32 * (h ^ 1)
                    sp.dma_start(zsw[32 * h:32 * h + 32, :], zs[o:o + 32, :]).then_inc(swap_in, 16)

            def load_bias(l, un):
                b = un - DUNITS
                sp.wait_ge(m_ready, UNITS * l + (un - 1 if b >= 2 else DUNITS - 4))
                sp.dma_start(bias[:, b % 2, :], nabias[l, b]).then_inc(bias_in[b % 2], 16)

            sp.dma_start(par[:, :], prm[0]).then_inc(par_in, 16)
            sp.dma_start(x[:, 0:2, :], xT[:, 0:2, :]).then_inc(x_in, 16)
            load(0, 0, False)
            sp.dma_start(x[:, 2:KD, :], xT[:, 2:KD, :]).then_inc(x_in, 16)
            for c in range(1, RAW):
                load(0, c, False)
            sp.dma_start(cs[:, :, :], rope).then_inc(const_in, 16)
            sp.dma_start(cnt[:, :], lncnt).then_inc(const_in, 16)
            sp.dma_start(gf[:, :], gfin).then_inc(const_in, 16)
            for c in range(RAW, LOAD_AHEAD):
                load(0, c, True)
            for l in range(DEPTH):
                for c in range(PRE):
                    load_next(l, c)
                    if (r := rope_of(c)) is not None:
                        swap(l, r)
                for n in range(UNITS):
                    c, ends = tile_at(n)
                    if not ends:
                        load_next(l, c)
                    elif (r := rope_of(c)) is not None:
                        swap(l, r)
                    if n == DUNITS - 4:
                        load_bias(l, DUNITS)
                        load_bias(l, DUNITS + 1)
                    if DUNITS <= n < UNITS - 2:
                        load_bias(l, n + 2)
                for c in range(N_IN, N_CH):
                    load_next(l, c)
                    if c == N_IN + CT and l + 1 < DEPTH:
                        sp.wait_ge(ylo_ready, KD * (l + 1))
                        sp.dma_start(par[:, :], prm[l + 1]).then_inc(par_in, 16)
            for k in range(KD):
                sp.wait_ge(res_ready, k + 1)
                sp.dma_start(out[:, k, :], y[:, k, :]).then_inc(out_in, 16)
            sp.wait_ge(out_in, 16 * KD)

        @block.tensor
        def _(pe):
            def products(c, k_slice, a_hi, a_lo, ks, order=None, ready=None):
                slot, bankc, K = c % SPL, acc[c % 2], rows_of(c)
                for i in k_slice:
                    k = i if order is None else order[i]
                    if ready is not None:
                        pe.wait_ge(ready[0], ready[1] + i + 1)
                    nc.tensor.matmul(bankc[:, :], w_hi[:, slot, k, :], a_hi[:, k, :], start=i == 0, stop=False)
                    nc.tensor.matmul(bankc[:, :], w_lo[:, slot, k, :], a_hi[:, k, :], start=False, stop=False)
                    last = nc.tensor.matmul(bankc[:, :], w_hi[:, slot, k, :], a_lo[:, k, :], start=False, stop=i == K - 1)
                if k_slice[-1] == K - 1:
                    last.then_inc(tile_done, 1)

            def open_tile(l, c):
                pe.wait_ge(lo_ready, N_CH * l + c + 1)
                pe.wait_ge(acc_free, emptied(l, c - 2))

            def in_tile(l, c, half=None, ready=None):
                if half in (None, 0):
                    open_tile(l, c)
                ks = range(KD) if half is None else range(half * KD // 2, (half + 1) * KD // 2)
                products(c, list(ks), act_hi, act_lo, KD, ready=ready)

            def take_misc(l, k):
                pe.wait_ge(misc_free, MISC_L * l + k)

            def norm_col(l, k, adds):
                take_misc(l, k)
                pe.wait_ge(add_done, adds)
                for a in range(QT):
                    last = nc.tensor.matmul(misc[:, a:a + 1], ssq[:, a * P:(a + 1) * P], ones[:, 0:1],
                                            start=True, stop=True)
                last.then_inc(misc_ready, 1)

            def norm_bc(l, k, diags):
                take_misc(l, k)
                pe.wait_ge(diag_ready, diags)
                nc.tensor.matmul(misc[:, :], ones[:, :], diag[:, :, :].rearrange("p a t -> p (a t)"),
                                 start=True, stop=True).then_inc(misc_ready, 1)

            def scores(l, n):
                g, h, b = unit(n)
                if n % UPP == 0:
                    if g < DPAIRS:
                        pe.wait_ge(qk_ready, ROPES * l + 2 * g + 2)
                    else:
                        pe.wait_ge(acc_free, emptied(l, IN_TILES.index(("ak", g - DPAIRS))))
                if n >= 2:
                    pe.wait_ge(m_ready, UNITS * l + n - 1)
                q = qpad[:, g % 2, h, b * P:(b + 1) * P]
                if g < DPAIRS:
                    o, k = sc[n % 2][:, :], kT[:, g % 2, :]
                else:
                    o, k = sc[n % 2][:, 0:NKEY], kT[:, g % 2, ROWS * NA_LO[b]:ROWS * NA_LO[b] + NKEY]
                nc.tensor.matmul(o, q, k, start=True, stop=True).then_inc(s_ready, 1)

            def turn(l, n):
                g, h, b = unit(n)
                pe.wait_ge(p_ready, UNITS * l + n + 1)
                if n >= 2:
                    pe.wait_ge(pt_ready, UNITS * l + n - 1)
                blocks = QT if g < DPAIRS else NKEY // P
                for k in range(blocks):
                    last = nc.tensor.transpose(tp[n % 2][:, k * P:(k + 1) * P],
                                               prob[:, n % 3, k * P:(k + 1) * P], ident[:, :])
                last.then_inc(t_ready, 1)

            def turn_v(l, g, rnd):
                pe.wait_ge(acc_free, emptied(l, v_tile(g)))
                take_misc(l, MISC_V[g][rnd])
                for i in range(QT):
                    if g < DPAIRS:
                        src = vT[:, i * P:(i + 1) * P]
                    else:
                        b, half = divmod(rnd * QT + i, 2)
                        first = ROWS * NA_LO[b] + half * P
                        src = vT[:, first:first + P]
                    last = nc.tensor.transpose(misc[:, i * P:(i + 1) * P], src, ident[:, :])
                last.then_inc(misc_ready, 1)

            def values(l, g):
                pe.wait_ge(pt_ready, UNITS * l + UPP * (g + 1))
                pe.wait_ge(misc_free, MISC_L * l + MISC_V[g][-1] + 1)
                if g >= 1:
                    pe.wait_ge(pair_final, PAIRS * l + g)
                if g < DPAIRS:
                    for k in range(QT):
                        for h in range(2):
                            last = nc.tensor.matmul(ob[HD * h:HD * (h + 1), :], v[:, g % 2, k, HD * h:HD * (h + 1)],
                                                    pT[:, h, k, :], start=k == 0, stop=k == QT - 1)
                else:
                    for b in range(QT):
                        for half in range(2):
                            for h in range(2):
                                last = nc.tensor.matmul(ob[HD * h:HD * (h + 1), b * P:(b + 1) * P],
                                                        v[:, g % 2, 2 * b + half, HD * h:HD * (h + 1)],
                                                        pT[:, h, half, b * P:(b + 1) * P],
                                                        start=half == 0, stop=half == 1)
                last.then_inc(pv_done, 1)

            def ln_mean(l):
                take_misc(l, MISC_MEAN)
                pe.wait_ge(conv_step, STEPS * (l + 1))
                for j in range(CT):
                    last = nc.tensor.matmul(misc[:, :], mean_w[:, :], y[:, KD - CT + j, :], start=j == 0, stop=j == CT - 1)
                last.then_inc(misc_ready, 1)

            pe.wait_ge(consts, 5)
            for l in range(DEPTH):
                in_tile(l, 0, ready=(xlo_ready, KD * l))
                norm_col(l, MISC_COL, ADD_L * l + KD - 1)
                in_tile(l, 1)
                norm_bc(l, MISC_BC, 2 * l + 1)
                for c in range(2, PRE):
                    in_tile(l, c)
                for n in range(UNITS + 2):
                    if n < UNITS:
                        scores(l, n)
                        in_tile(l, tile_at(n)[0], n % 2)
                    else:
                        for c in ([N_IN, N_IN + 1] if n == UNITS else [N_IN + 2]):
                            open_tile(l, c)
                            pe.wait_ge(slo_ready, CT * (l + 1))
                            products(c, list(range(CT)), s_hi, s_lo, CT)
                    if n >= UPP + 1 and n % UPP == 1:
                        values(l, n // UPP - 1)
                    if 1 <= n <= UNITS:
                        turn(l, n - 1)
                    for g, rnd in V_AT.get(n, ()):
                        turn_v(l, g, rnd)
                    if n == LN_MEAN:
                        ln_mean(l)
                    if n == LN_COL:
                        norm_col(l, MISC_LCOL, ADD_L * (l + 1))
                    if n == LN_BC:
                        norm_bc(l, MISC_LBC, 2 * l + 2)
                for c in range(N_IN + CT, N_CH):
                    open_tile(l, c)
                    ready = (ylo_ready, KD * l) if c == N_IN + CT else None
                    products(c, list(range(KD)), act_hi, act_lo, KD, order=K_ORDER, ready=ready)
            norm_col(DEPTH, 0, ADD_L * DEPTH + KD - 1)
            norm_bc(DEPTH, 1, 2 * DEPTH + 1)

        @block.scalar
        def _(act):
            def split_hi(l, c):
                K = rows_of(c)
                if N_CH * l + c >= SPL:
                    act.wait_ge(tile_done, N_CH * l + c - SPL + 1)
                act.wait_ge(raw_in[c % RAW], 16 * (N_CH // RAW * l + c // RAW + 1))
                nc.scalar.activation(w_hi[:, c % SPL, 0:K, :], raw[:, c % RAW, 0:K, :], ACT.Copy).then_inc(hi_ready, 1)

            def split_next(l, c):
                if (f := follows(l, c + AHEAD)) is not None:
                    split_hi(*f)

            def squares(l, k):
                act.wait_ge(acc_free, x_tile(l, k))
                if k >= 2:
                    act.wait_ge(add_done, ADD_L * l + max(1, k - 2))
                nc.scalar.activation(sq[:, k % 2, :], x[:, k, :], ACT.Square).then_inc(sq_ready, 1)

            def ln_squares(l, j):
                act.wait_ge(misc_free, MISC_L * l + MISC_MEAN + 1)
                if j >= 2:
                    act.wait_ge(add_done, ADD_L * l + KD - 1 + 1)
                nc.scalar.activation(sq[:, j % 2, :], y[:, KD - CT + j, :], ACT.Square).then_inc(sq_ready, 1)

            def x_hi(l, k):
                act.wait_ge(acc_free, x_tile(l, k))
                nc.scalar.activation(act_hi[:, k, :], x[:, k, :], ACT.Copy,
                                     scale=par[:, P_G + k:P_G + k + 1]).then_inc(xhi_ready, 1)

            def tanh(l, key, src):
                i = TH_SEQ.index(key)
                act.wait_ge(th_used, TH_L * l + i)
                nc.scalar.activation(th[:, :], src, ACT.Tanh).then_inc(th_ready, 1)

            def exps(l, n):
                w = SEQ if n < DUNITS else NKEY
                act.wait_ge(m_ready, UNITS * l + n + 1)
                nc.scalar.activation(prob[:, n % 3, 0:w], prob[:, n % 3, 0:w], ACT.Exp, scale=-1.0,
                                     bias=nmx[:, n % 4:n % 4 + 1],
                                     accum_out=den[:, n % 4:n % 4 + 1]).then_inc(e_ready, 1)

            def empty_turn(l, n):
                g, h, b = unit(n)
                act.wait_ge(t_ready, UNITS * l + n + 1)
                if n % UPP == 0 and g:
                    act.wait_ge(pv_done, PAIRS * l + g)
                kk = QT if g < DPAIRS else NKEY // P
                nc.scalar.activation(pT[:, h, 0:kk, b * P:(b + 1) * P],
                                     tp[n % 2][:, 0:kk * P].rearrange("p (k t) -> p k t", t=P),
                                     ACT.Copy).then_inc(pt_ready, 1)

            def v_out(l, g, rnd):
                if g >= 2:
                    act.wait_ge(pv_done, PAIRS * l + g - 1)
                act.wait_ge(misc_ready, MISC_L * l + MISC_V[g][rnd] + 1)
                nc.scalar.activation(v[:, g % 2, rnd * QT:(rnd + 1) * QT, :],
                                     misc[:, :].rearrange("p (k t) -> p k t", t=P), ACT.Copy).then_inc(misc_free, 1)

            split_hi(0, 0)
            for k in range(KD - 1):
                squares(0, k)
            for c in range(1, AHEAD):
                split_hi(0, c)
            for l in range(DEPTH):
                act.wait_ge(par_in, 16 * (l + 1))
                if l:
                    act.wait_ge(tile_done, N_CH * l)
                for k in range(KD):
                    x_hi(l, k)
                    if k == 1:
                        squares(l, KD - 1)
                for c in range(PRE):
                    split_next(l, c)
                    kind, j = IN_TILES[c]
                    if kind == "cb":
                        mid = u[:, j, HALO:HALO + SEQ]
                        act.wait_ge(acc_free, emptied(l, c))
                        nc.scalar.activation(mid, mid, ACT.Tanh).then_inc(cbt_ready, 1)
                for n in range(UNITS + 2):
                    if n >= 2:
                        empty_turn(l, n - 2)
                    if n < UNITS:
                        exps(l, n)
                        if n % 2 == 0:
                            split_next(l, tile_at(n)[0])
                    else:
                        for c in ([N_IN, N_IN + 1] if n == UNITS else [N_IN + 2]):
                            split_next(l, c)
                    for g, rnd in V_AT.get(n - 1, ()):
                        v_out(l, g, rnd)
                    if n == LN_MEAN + 1:
                        for j in range(CT):
                            ln_squares(l, j)
                    if 0 < n - LN_SILU <= CT:
                        j = n - LN_SILU - 1
                        act.wait_ge(th_used, TH_L * l + TH_SEQ.index(("ln", j)) + 1)
                        nc.scalar.activation(s_hi[:, j, :], y[:, KD - CT + j, :], ACT.Copy).then_inc(shi_ready, 1)
                    if 0 <= n - LN_SILU < CT:
                        j = n - LN_SILU
                        act.wait_ge(hn_ready, CT * (l + 1))
                        tanh(l, ("ln", j), y[:, KD - CT + j, :])
                    if n and n % 2 == 0:
                        c = tile_at(n - 1)[0]
                        kind, j = IN_TILES[c]
                        if kind in Y_OF_GATE:
                            act.wait_ge(acc_free, emptied(l, c))
                            tanh(l, (kind, j), y[:, Y_OF_GATE[kind] + j, :])
                act.wait_ge(tile_done, N_CH * l + N_IN)
                for k in K_ORDER:
                    if k >= KD - CT:
                        act.wait_ge(acc_free, emptied(l, N_IN + k - (KD - CT)))
                    else:
                        act.wait_ge(pair_final, PAIRS * l + Y_OF_PAIR.index(k) + 1)
                    nc.scalar.activation(act_hi[:, k, :], y[:, k, :], ACT.Copy).then_inc(yhi_ready, 1)
                for c in range(N_IN + CT, N_CH):
                    split_next(l, c)
                    if c > N_IN + CT:
                        squares(l + 1, c - (N_IN + CT) - 1)
            squares(DEPTH, KD - 1)

        @block.gpsimd
        def _(pool):
            def split_lo(l, c):
                K = rows_of(c)
                pool.wait_ge(hi_ready, N_CH * l + c + 1)
                nc.gpsimd.tensor_tensor(w_lo[:, c % SPL, 0:K, :], raw[:, c % RAW, 0:K, :],
                                        w_hi[:, c % SPL, 0:K, :], ALU.subtract).then_inc(lo_ready, 1)

            def split_next(l, c):
                if (f := follows(l, c + AHEAD)) is not None:
                    split_lo(*f)

            def add_squares(l, k, base=0):
                sqs, adds = (SQ_L * l, ADD_L * l) if base == 0 else (SQ_L * l + KD, ADD_L * l + KD - 1)
                pool.wait_ge(sq_ready, sqs + k + 1)
                if k >= 2:
                    pool.wait_ge(add_done, adds + k - 1)
                a = sq[:, 0, :] if k == 1 else ssq[:, :]
                nc.gpsimd.tensor_tensor(ssq[:, :], a, sq[:, k % 2, :], ALU.add).then_inc(add_done, 1)

            def root(l, k):
                pool.wait_ge(misc_free, MISC_L * l + k + 1)
                nc.gpsimd.tensor_tensor(rcol[:, :], col[:, :], nhalf[:, :], ALU.pow).then_inc(pow_ready, 1)

            def norm(l, n):
                w = SEQ if n < DUNITS else NKEY
                pool.wait_ge(r_ready, UNITS * l + n + 1)
                nc.gpsimd.tensor_scalar(prob[:, n % 3, 0:w], prob[:, n % 3, 0:w], rden[:, n % 4:n % 4 + 1],
                                        1.0, ALU.mult, ALU.mult).then_inc(p_ready, 1)

            def rotate(l, r):
                pool.wait_ge(swap_in, 64 * (ROPES * l + r + 1))
                nc.gpsimd.tensor_tensor(zsw[:, :], zsw[:, :], cs[:, 1, :], ALU.mult).then_inc(t2_ready, 1)

            nc.gpsimd.memset(ident[:, :], 0.0).then_inc(consts, 1)
            nc.gpsimd.memset(ones[:, :], 1.0).then_inc(consts, 1)
            nc.gpsimd.memset(mean_w[:, :], 1.0 / CONV_CH).then_inc(consts, 1)
            nc.gpsimd.memset(nhalf[:, :], -0.5).then_inc(consts, 1)
            pool.wait_ge(consts, 4)
            nc.gpsimd.affine_select(out=ident[:, :], in_=ident[:, :], compare_op=ALU.not_equal, fill=1.0, base=0,
                                    pattern=[[-1, P]], channel_multiplier=1).then_inc(consts, 1)
            pool.wait_ge(const_in, 48)
            split_lo(0, 0)
            for k in range(1, KD - 1):
                add_squares(0, k)
            for c in range(1, AHEAD):
                split_lo(0, c)
            for l in range(DEPTH):
                add_squares(l, KD - 1)
                root(l, MISC_COL)
                for c in range(PRE):
                    split_next(l, c)
                    if (r := rope_of(c)) is not None:
                        rotate(l, r)
                for n in range(UNITS + 1):
                    if n:
                        norm(l, n - 1)
                    if n < UNITS and n % 2 == 0:
                        split_next(l, tile_at(n)[0])
                    if n and n % 2 == 0:
                        if (r := rope_of(tile_at(n - 1)[0])) is not None:
                            rotate(l, r)
                    if n == LN_MEAN + 1:
                        for j in range(1, CT):
                            add_squares(l, j, base=1)
                    if n == LN_BC:
                        root(l, MISC_LCOL)
                for c in range(N_IN, N_CH):
                    split_next(l, c)
                    if c >= N_IN + CT + 2:
                        add_squares(l + 1, c - (N_IN + CT) - 1)
            add_squares(DEPTH, KD - 1)
            root(DEPTH, MISC_COL)

        @block.vector
        def _(dve):
            own = [0]

            def step(ins):
                own[0] += 1
                ins.then_inc(dve_own, 1)
                dve.wait_ge(dve_own, own[0])

            def column(l, k, width):
                dve.wait_ge(misc_ready, MISC_L * l + k + 1)
                nc.vector.tensor_scalar(col[:, :], misc[:, 0:QT], 1.0 / width, EPS, ALU.mult, ALU.add)\
                    .then_inc(misc_free, 1)

            def diagonals(i):
                dve.wait_ge(pow_ready, i + 1)
                for a in range(QT):
                    last = nc.vector.tensor_scalar(diag[:, a, :], ident[:, :], rcol[:, a:a + 1], None, ALU.mult)
                last.then_inc(diag_ready, 1)

            def take_factor(l):
                dve.wait_ge(misc_ready, MISC_L * l + MISC_BC + 1)
                nc.vector.tensor_copy(rstd[:, :], misc[:, :]).then_inc(misc_free, 1)
                dve.wait_ge(misc_free, MISC_L * l + MISC_BC + 1)

            def scaled(dst, c, factor):
                return nc.vector.scalar_tensor_tensor(out=dst, in0=acc[c % 2][:, :], scalar=factor, in1=rstd[:, :],
                                                      op0=ALU.mult, op1=ALU.mult)

            def scaled_by_column(dst, c, factor):
                def view(a):
                    return a.rearrange("p (r c) -> p r c", c=GRID_W)
                return nc.vector.scalar_tensor_tensor(out=dst.rearrange("p (c r) -> p r c", c=GRID_W),
                                                      in0=view(acc[c % 2][:, :]), scalar=factor, in1=view(rstd[:, :]),
                                                      op0=ALU.mult, op1=ALU.mult)

            def empty_tile(l, c):
                kind, j = IN_TILES[c]
                dve.wait_ge(tile_done, N_CH * l + c + 1)
                if kind == "cb":
                    scaled(u[:, j, HALO:HALO + SEQ], c, 0.5).then_inc(acc_free, 1)
                elif kind == "ca":
                    half = y[:, KD - CT + j, :]
                    scaled(half, c, 0.5).then_inc(acc_free, 1)
                    dve.wait_ge(acc_free, emptied(l, c))
                    dve.wait_ge(cbt_ready, CT * l + j + 1)
                    mid = u[:, j, HALO:HALO + SEQ]
                    nc.vector.scalar_tensor_tensor(out=mid, in0=mid, scalar=1.0, in1=half, op0=ALU.add,
                                                   op1=ALU.mult).then_inc(u_ready, 1)
                elif kind in ("bq", "bk"):
                    scaled(zs[:, :], c, HD ** -0.5 if kind == "bq" else 1.0).then_inc(acc_free, 1)
                    dve.wait_ge(acc_free, emptied(l, c))
                    nc.vector.tensor_tensor(zc[:, :], zs[:, :], cs[:, 0, :], ALU.mult).then_inc(dve_own, 1)
                    own[0] += 1
                elif kind in ("bv", "av"):
                    g = j if kind == "bv" else DPAIRS + j
                    if g:
                        dve.wait_ge(misc_free, MISC_L * l + MISC_V[g - 1][-1] + 1)
                    (scaled if kind == "bv" else scaled_by_column)(vT[:, :], c, 1.0).then_inc(acc_free, 1)
                elif kind == "aq":
                    g = DPAIRS + j
                    for h in range(2):
                        o = HD * h
                        dst = qpad[o:o + HD, g % 2, h, :].rearrange("p (b r c) -> p r b c", b=QT, r=ROWS)
                        src = acc[c % 2][o:o + HD, :].rearrange("p (r b c) -> p r b c", b=QT, r=ROWS)
                        fac = rstd[o:o + HD, :].rearrange("p (r b c) -> p r b c", b=QT, r=ROWS)
                        last = nc.vector.tensor_tensor(dst, src, fac, ALU.mult)
                    last.then_inc(acc_free, 1)
                elif kind == "ak":
                    scaled_by_column(kT[:, (DPAIRS + j) % 2, :], c, HD ** -0.5).then_inc(acc_free, 1)
                else:
                    scaled(y[:, Y_OF_GATE[kind] + j, :], c, 0.5).then_inc(acc_free, 1)

            def rotated(l, r):
                g = r // 2
                dve.wait_ge(t2_ready, ROPES * l + r + 1)
                dve.wait_ge(dve_own, own[0])
                if r % 2:
                    last = nc.vector.tensor_tensor(kT[:, g % 2, :], zc[:, :], zsw[:, :], ALU.add)
                else:
                    for h in range(2):
                        o = HD * h
                        last = nc.vector.tensor_tensor(qpad[o:o + HD, g % 2, h, :], zc[o:o + HD, :],
                                                       zsw[o:o + HD, :], ALU.add)
                last.then_inc(qk_ready, 1)

            def conv_taps(l, first, count):
                for i in range(first, min(first + count, STEPS)):
                    j, t = divmod(i, TAPS + 1)
                    dst = (y[:, KD - CT + j, :], acc2[:, :])[t % 2]
                    if t == 0:
                        dve.wait_ge(u_ready, CT * l + j + 1)
                    if STEPS * l + i:
                        dve.wait_ge(conv_step, STEPS * l + (i if t == TAPS or t < 2 else i - 1))
                    src = u[:, j, t % TAPS:t % TAPS + SEQ]
                    w = par[:, P_W + TAPS * j + t % TAPS:P_W + TAPS * j + t % TAPS + 1]
                    if t == 0:
                        ins = nc.vector.tensor_scalar(dst, src, w, par[:, P_B + j:P_B + j + 1], ALU.mult, ALU.add)
                    elif t == 1:
                        ins = nc.vector.tensor_scalar(dst, src, w, None, ALU.mult)
                    elif t < TAPS:
                        ins = nc.vector.scalar_tensor_tensor(out=dst, in0=src, scalar=w, in1=dst, op0=ALU.mult,
                                                             op1=ALU.add)
                    else:
                        a = y[:, KD - CT + j, :]
                        ins = nc.vector.tensor_tensor(a, a, acc2[:, :], ALU.add)
                    ins.then_inc(conv_step, 1)

            def maxima(l, n):
                g, h, b = unit(n)
                dve.wait_ge(s_ready, UNITS * l + n + 1)
                if n >= 3:
                    dve.wait_ge(t_ready, UNITS * l + n - 2)
                if g < DPAIRS:
                    w, add = SEQ, cnt[:, P * (QT - 1 - b):P * (QT - 1 - b) + SEQ]
                else:
                    w, i = NKEY, n - DUNITS
                    dve.wait_ge(bias_in[i % 2], 16 * (UPP * l + i // 2 + 1))
                    add = bias[:, i % 2, :]
                nc.vector.tensor_tensor_reduce(out=prob[:, n % 3, 0:w], in0=sc[n % 2][:, 0:w], in1=add, scale=-1.0,
                                               scalar=3e38, op0=ALU.add, op1=ALU.min,
                                               accum_out=nmx[:, n % 4:n % 4 + 1]).then_inc(m_ready, 1)

            def reciprocal(l, n):
                dve.wait_ge(e_ready, UNITS * l + n + 1)
                nc.vector.reciprocal(rden[:, n % 4:n % 4 + 1], den[:, n % 4:n % 4 + 1]).then_inc(r_ready, 1)

            def silu(l, key, t):
                dve.wait_ge(th_ready, TH_L * l + TH_SEQ.index(key) + 1)
                nc.vector.scalar_tensor_tensor(out=t, in0=th[:, :], scalar=1.0, in1=t, op0=ALU.add,
                                               op1=ALU.mult).then_inc(th_used, 1)

            def gated(l, g):
                dve.wait_ge(pv_done, PAIRS * l + g + 1)
                gate = ("bg", g) if g < DPAIRS else ("ag", g - DPAIRS)
                dve.wait_ge(th_used, TH_L * l + TH_SEQ.index(gate) + 1)
                t = y[:, Y_OF_PAIR[g], :]
                if g < DPAIRS:
                    ins = nc.vector.tensor_tensor(t, ob[:, :], t, ALU.mult)
                else:
                    t = t.rearrange("p (r b c) -> p r b c", b=QT, r=ROWS)
                    o = ob[:, :].rearrange("p (b r c) -> p r b c", b=QT, r=ROWS)
                    ins = nc.vector.tensor_tensor(t, o, t, ALU.mult)
                ins.then_inc(pair_final, 1)

            nc.vector.memset(u[:, :, :], 0.0).then_inc(cleared, 1)
            nc.vector.memset(qpad[:, :, :, :], 0.0).then_inc(cleared, 1)
            dve.wait_ge(cleared, 2)
            dve.wait_ge(x_in, 32)
            dve.wait_ge(const_in, 48)
            dve.wait_ge(consts, 5)
            nc.vector.memset(nmx[:, :], 0.0).then_inc(acc_free, ACC0)
            for l in range(DEPTH):
                dve.wait_ge(par_in, 16 * (l + 1))
                step(nc.vector.tensor_scalar(parh[:, :], par[:, P_LG:P_LG + 2 * CT], 0.5, None, ALU.mult))
                for k in range(KD):
                    dve.wait_ge(xhi_ready, KD * l + k + 1)
                    nc.vector.scalar_tensor_tensor(out=act_lo[:, k, :], in0=x[:, k, :],
                                                   scalar=par[:, P_G + k:P_G + k + 1], in1=act_hi[:, k, :],
                                                   op0=ALU.mult, op1=ALU.subtract).then_inc(xlo_ready, 1)
                column(l, MISC_COL, D)
                diagonals(2 * l)
                take_factor(l)
                taps = 0
                for c in range(PRE):
                    empty_tile(l, c)
                    if c >= 1:
                        conv_taps(l, taps, PRE_TAPS)
                        taps += PRE_TAPS
                    if c and (r := rope_of(c - 1)) is not None:
                        pass
                    if (r := rope_of(c)) is not None:
                        rotated(l, r)
                for n in range(UNITS + 2):
                    if n < UNITS:
                        maxima(l, n)
                    if 0 < n <= UNITS:
                        reciprocal(l, n - 1)
                    if n >= UPP + 2 and n % UPP == 2:
                        gated(l, n // UPP - 1)
                    if n and n % 2 == 1:
                        c = tile_at(n - 2)[0] if n >= 2 else 0
                        if n >= 2 and IN_TILES[c][0] in Y_OF_GATE:
                            kind, j = IN_TILES[c]
                            silu(l, (kind, j), y[:, Y_OF_GATE[kind] + j, :])
                        if n >= 2 and (r := rope_of(c)) is not None:
                            rotated(l, r)
                    if n and n % 2 == 0:
                        empty_tile(l, tile_at(n - 1)[0])
                    conv_taps(l, taps, SLOT_TAPS)
                    taps += SLOT_TAPS
                    if n == LN_MEAN:
                        dve.wait_ge(misc_ready, MISC_L * l + MISC_MEAN + 1)
                        for j in range(CT):
                            t = y[:, KD - CT + j, :]
                            last = nc.vector.tensor_tensor(t, t, misc[:, :], ALU.subtract)
                        last.then_inc(misc_free, 1)
                    if n == LN_COL:
                        column(l, MISC_LCOL, CONV_CH)
                    if n == LN_BC:
                        diagonals(2 * l + 1)
                        dve.wait_ge(misc_ready, MISC_L * l + MISC_LBC + 1)
                        for j in range(CT):
                            t = y[:, KD - CT + j, :]
                            last = nc.vector.tensor_tensor(t, t, misc[:, :], ALU.mult)
                        last.then_inc(misc_free, 1)
                        dve.wait_ge(misc_free, MISC_L * l + MISC_LBC + 1)
                        for j in range(CT):
                            t = y[:, KD - CT + j, :]
                            nc.vector.tensor_scalar(t, t, parh[:, j:j + 1], parh[:, CT + j:CT + j + 1], ALU.mult,
                                                    ALU.add).then_inc(hn_ready, 1)
                    if 0 <= n - LN_SILU < CT:
                        j = n - LN_SILU
                        silu(l, ("ln", j), y[:, KD - CT + j, :])
                    if 0 < n - LN_SILU <= CT:
                        j = n - LN_SILU - 1
                        dve.wait_ge(shi_ready, CT * l + j + 1)
                        nc.vector.tensor_tensor(s_lo[:, j, :], y[:, KD - CT + j, :], s_hi[:, j, :], ALU.subtract)\
                            .then_inc(slo_ready, 1)
                dve.wait_ge(th_used, TH_L * (l + 1))
                for j in range(CT):
                    if j == CT - 1:
                        gated(l, PAIRS - 1)
                    dve.wait_ge(tile_done, N_CH * l + N_IN + j + 1)
                    t = y[:, KD - CT + j, :]
                    nc.vector.scalar_tensor_tensor(out=t, in0=acc[(N_IN + j) % 2][:, :],
                                                   scalar=par[:, P_PB + j:P_PB + j + 1], in1=t, op0=ALU.add,
                                                   op1=ALU.mult).then_inc(acc_free, 1)
                for i, k in enumerate(K_ORDER):
                    dve.wait_ge(yhi_ready, KD * l + i + 1)
                    nc.vector.tensor_tensor(act_lo[:, k, :], y[:, k, :], act_hi[:, k, :], ALU.subtract)\
                        .then_inc(ylo_ready, 1)
                for k in range(KD):
                    c = N_IN + CT + k
                    dve.wait_ge(tile_done, N_CH * l + c + 1)
                    nc.vector.tensor_tensor(x[:, k, :], x[:, k, :], acc[c % 2][:, :], ALU.add).then_inc(acc_free, 1)
            column(DEPTH, MISC_COL, D)
            diagonals(2 * DEPTH)
            take_factor(DEPTH)
            for k in range(KD):
                nc.vector.scalar_tensor_tensor(out=y[:, k, :], in0=x[:, k, :], scalar=gf[:, k:k + 1],
                                               in1=rstd[:, :], op0=ALU.mult, op1=ALU.mult).then_inc(res_ready, 1)


def by_partition(a):
    *lead, r, c = a.shape
    a = a.reshape(*lead, r // P, P, c // P, P)
    n = len(lead)
    return a.transpose(*range(n), n + 2, n + 1, n, n + 3)


def dil_table():
    diff = np.arange(NEG_TILE)[None, :] - P * (QT - 1) - np.arange(P)[:, None]
    count = np.zeros(diff.shape, np.int64)
    for w, d in PATTERNS:
        count += (np.abs(diff) <= (w // 2) // d * d) & (diff % d == 0)
    return np.where(count > 0, np.log(np.maximum(count, 1)), NEG).astype(np.float32)


def rope_table():
    half = HD // 2
    ang = np.arange(SEQ)[None, :] * 10000.0 ** (-np.arange(half) * 2.0 / HD)[:, None]
    cos, sin = np.cos(ang), np.sin(ang)
    out = np.stack([np.tile(cos, (4, 1)), np.concatenate([-sin, sin, -sin, sin])], 1)
    return np.ascontiguousarray(out.astype(np.float32))


def na_bias(rpb):
    b, r, c = np.meshgrid(np.arange(QT), np.arange(ROWS), np.arange(GRID_W // QT), indexing="ij")
    col = (GRID_W // QT * b + c).reshape(QT, P)
    row = r.reshape(QT, P)
    j, i = np.meshgrid(np.arange(NAW), np.arange(ROWS), indexing="ij")
    i, j = i.ravel(), j.ravel()
    key_col = np.array(NA_LO)[:, None] + j[None, :]
    first = np.clip(col - WIN_COLS // 2, 0, GRID_W - WIN_COLS)
    inside = (key_col[:, None, :] >= first[:, :, None]) & (key_col[:, None, :] < first[:, :, None] + WIN_COLS)
    at_r = i[None, None, :] - row[:, :, None] + ROWS - 1
    at_c = np.clip(key_col[:, None, :] - col[:, :, None] + WIN_COLS - 1, 0, 2 * WIN_COLS - 2)
    full = np.where(inside, rpb[:, :, at_r, at_c], np.float32(NEG))
    L = rpb.shape[0]
    full = full.reshape(L, NA_HEADS // 2, 2, QT, P, NKEY).transpose(0, 1, 3, 2, 4, 5)
    return np.ascontiguousarray(full.reshape(L, 2 * UPP, P, NKEY))


def kernel(x, norm_g, w_in, na_rpb, conv_w, conv_b, conv_ln_g, conv_ln_b, pw_w, pw_b, w_out, final_g):
    import concourse.bacc as bacc
    from concourse.bass_utils import run_bass_kernel_spmd

    x, norm_g, w_in, na_rpb, conv_w, conv_b, conv_ln_g, conv_ln_b, pw_w, pw_b, w_out, final_g = map(
        np.asarray, (x, norm_g, w_in, na_rpb, conv_w, conv_b, conv_ln_g, conv_ln_b, pw_w, pw_b, w_out, final_g))

    def tiles(a):
        return a.reshape(DEPTH, -1, P).transpose(0, 2, 1)

    order = [PART_AT[kind] // P + j for kind, j in IN_TILES]
    taps = conv_w.transpose(0, 2, 1).reshape(DEPTH, CT, P, TAPS).transpose(0, 2, 1, 3).reshape(DEPTH, P, CT * TAPS)
    arrays = {
        "xT": x[0].T.reshape(KD, P, SEQ).transpose(1, 0, 2),
        "w_in": by_partition(w_in)[:, order],
        "w_pw": by_partition(pw_w),
        "w_out": by_partition(w_out),
        "prm": np.concatenate([tiles(norm_g), taps, tiles(conv_b), tiles(conv_ln_g), tiles(conv_ln_b), tiles(pw_b)], 2),
        "gfin": final_g.reshape(KD, P).T,
        "nabias": na_bias(na_rpb),
        "lncnt": dil_table(),
        "rope": rope_table(),
    }
    arrays = {k: np.ascontiguousarray(a) for k, a in arrays.items()}
    nc = bacc.Bacc("TRN2", target_bir_lowering=False, num_devices=1)
    aps = [nc.dram_tensor(k, a.shape, mybir.dt.from_np(a.dtype), kind="ExternalInput").ap() for k, a in arrays.items()]
    aps.append(nc.dram_tensor("out", (P, KD, SEQ), F32, kind="ExternalOutput").ap())
    build(nc, *aps)
    got = run_bass_kernel_spmd(nc, [arrays], core_ids=[0]).results[0]["out"]
    return got.transpose(1, 0, 2).reshape(D, SEQ).T.reshape(1, SEQ, D)
```

```python
from contextlib import ExitStack

import numpy as np
import concourse.bass as bass
from concourse import mybir

F32 = mybir.dt.float32
F32R = mybir.dt.float32r
ALU = mybir.AluOpType
ACT = mybir.ActivationFunctionType

P = 128
SEQ = 512
D = 1024
DEPTH = 2
GRID_W = 64
ROWS = SEQ // GRID_W
HD = 64
NA_HEADS, DIL_HEADS = 4, 6
WIN_COLS = 16
PATTERNS = ((128, 1), (512, 4), (2048, 16))
CONV_CH = 384
TAPS = 31
HALO = TAPS // 2
EPS = 1e-6
NEG = -1e30
KD = D // P
CT = CONV_CH // P
QT = SEQ // P

IN_TILES = [("cb", 0), ("ca", 0), ("bq", 0), ("cb", 1), ("bk", 0), ("ca", 1), ("cb", 2), ("ca", 2), ("bq", 1),
            ("bv", 0), ("bk", 1), ("bg", 0), ("bq", 2),
            ("bv", 1), ("bk", 2), ("bg", 1), ("bv", 2),
            ("aq", 0), ("ak", 0), ("av", 0), ("bg", 2),
            ("aq", 1), ("ak", 1), ("av", 1), ("ag", 0),
            ("ag", 1), ("cg", 0), ("cg", 1), ("cg", 2)]
PART_AT = {"aq": 0, "ak": 256, "av": 512, "ag": 768, "bq": 1024, "bk": 1408, "bv": 1792, "bg": 2176,
           "ca": 2560, "cb": 2944, "cg": 3328}
N_IN = len(IN_TILES)
PRE = 9
N_CH = N_IN + CT + KD
RAW = 4
SPL = 4
AHEAD = SPL - 1
LOAD_AHEAD = AHEAD + RAW
assert N_CH % RAW == 0 and N_CH % SPL == 0

PAIRS = 5
DPAIRS = DIL_HEADS // 2
UPP = 8
UNITS = PAIRS * UPP
LAG = 2
PROBS = LAG + 2
SLOTS = UNITS + LAG + 1
DUNITS = DPAIRS * UPP
Y_OF_PAIR = [2, 3, 4, 0, 1]
K_ORDER = [2, 3, 4, 0, 5, 6, 1, 7]
NAW = 32
NA_LO = [0, 8, 24, 32]
NKEY = ROWS * NAW
NEG_TILE = 896
PREP = 8 + CT * TAPS + 4 * CT
P_G, P_W, P_B = 0, 8, 8 + CT * TAPS
P_LG, P_LB, P_PB = P_B + CT, P_B + 2 * CT, P_B + 3 * CT

X_BEFORE_W1 = 4

LN_SUM, LN_MEAN, LN_COL, LN_BC, LN_SILU = 19, 20, 23, 26, 28
X_LATE = 6
PRE_TAPS, SLOT_TAPS = 5, 3


def unit(n):
    return n // UPP, n % 2, (n % UPP) // 2


def build(nc, xT, w_in, w_pw, w_out, prm, gfin, nabias, lncnt, rope, out):
    with ExitStack() as ctx:
        def sb(name, shape, dt=F32):
            return ctx.enter_context(nc.sbuf_tensor(name, shape, dt))

        def bank(name):
            return ctx.enter_context(nc.psum_tensor(name, [P, SEQ], F32))

        def sem(name):
            return ctx.enter_context(nc.semaphore(name))

        x = sb("x", [P, KD, SEQ])
        act_hi = sb("act_hi", [P, KD, SEQ], F32R)
        act_lo = sb("act_lo", [P, KD, SEQ], F32R)
        y = sb("y", [P, KD, SEQ])
        raw = sb("raw", [P, RAW, KD, P])
        w_hi = sb("w_hi", [P, SPL, KD, P], F32R)
        w_lo = sb("w_lo", [P, SPL, KD, P], F32R)
        qpad = sb("qpad", [P, 2, 2, SEQ])
        kT = sb("kT", [P, 2, SEQ])
        v = sb("v", [P, 2, 2 * QT, P])
        vT = sb("vT", [P, SEQ])
        zs = sb("zs", [P, SEQ])
        zsw = sb("zsw", [P, SEQ])
        zc = sb("zc", [P, SEQ])
        u = sb("u", [P, CT, SEQ + 2 * HALO])
        acc2 = sb("acc2", [P, SEQ])
        s_hi = sb("s_hi", [P, CT, SEQ], F32R)
        s_lo = sb("s_lo", [P, CT, SEQ], F32R)
        th = sb("th", [P, SEQ])
        prob = sb("prob", [P, PROBS, SEQ])
        pT = sb("pT", [P, 2, QT, SEQ])
        bias = sb("bias", [P, 2, NKEY])
        sq = sb("sq", [P, 2, SEQ])
        ssq = sb("ssq", [P, SEQ])
        rstd = sb("rstd", [P, SEQ])
        diag = acc2[:, :].rearrange("p (a t) -> p a t", a=QT)
        cnt = sb("cnt", [P, NEG_TILE])
        cs = sb("cs", [P, 2, SEQ])
        ident = sb("ident", [P, P])
        ones = sb("ones", [P, P])
        mean_w = sb("mean_w", [P, P])
        par = sb("par", [P, PREP])
        parh = sb("parh", [P, 2 * CT])
        gf = sb("gf", [P, KD])
        nmx = sb("nmx", [P, 4])
        den = sb("den", [P, 4])
        rden = sb("rden", [P, 4])
        col = sb("col", [P, QT])
        rcol = sb("rcol", [P, QT])
        nhalf = sb("nhalf", [P, QT])

        acc = [bank("acc0"), bank("acc1")]
        sc = [bank("sc0"), bank("sc1")]
        tp = [bank("tp0"), bank("tp1")]
        ob = bank("ob")
        misc = bank("misc")

        raw_in = [sem(f"raw_in{i}") for i in range(RAW)]
        x_in = [sem(f"x_in{k}") for k in range(KD)]
        const_in = sem("const_in")
        par_in = sem("par_in")
        bias_in = [sem(f"bias_in{i}") for i in range(2)]
        swap_in = sem("swap_in")
        out_in = sem("out_in")
        consts = sem("consts")
        cleared = sem("cleared")
        hi_ready = sem("hi_ready")
        lo_ready = sem("lo_ready")
        xhi_ready = sem("xhi_ready")
        xlo_ready = sem("xlo_ready")
        yhi_ready = sem("yhi_ready")
        ylo_ready = sem("ylo_ready")
        tile_done = sem("tile_done")
        act_used = sem("act_used")
        acc_free = sem("acc_free")
        sq_ready = sem("sq_ready")
        add_done = sem("add_done")
        misc_ready = sem("misc_ready")
        misc_free = sem("misc_free")
        pow_ready = sem("pow_ready")
        diag_ready = sem("diag_ready")
        cbt_ready = sem("cbt_ready")
        u_ready = sem("u_ready")
        conv_step = sem("conv_step")
        t2_ready = sem("t2_ready")
        qk_ready = sem("qk_ready")
        s_ready = sem("s_ready")
        m_ready = sem("m_ready")
        e_ready = sem("e_ready")
        r_ready = sem("r_ready")
        p_ready = sem("p_ready")
        t_ready = sem("t_ready")
        pt_ready = sem("pt_ready")
        pv_done = sem("pv_done")
        pair_final = sem("pair_final")
        th_ready = sem("th_ready")
        th_used = sem("th_used")
        hn_ready = sem("hn_ready")
        shi_ready = sem("shi_ready")
        slo_ready = sem("slo_ready")
        dve_own = sem("dve_own")
        res_ready = sem("res_ready")

        MISC_COL, MISC_BC = 0, 1
        MISC_V = {0: [2], 1: [3], 2: [4], 3: [7, 9], 4: [10, 11]}
        MISC_MEAN, MISC_LCOL, MISC_LBC = 5, 6, 8
        MISC_L = 12
        V_AT = {3: (0, 0), 10: (1, 0), 17: (2, 0), 25: (3, 0), 27: (3, 1), 34: (4, 0), 36: (4, 1)}
        ROPES = 2 * DPAIRS
        ADD_L = (KD - 1) + 2 * (CT - 1)
        LN_ADDS = KD - 1 + CT - 1
        SQ_L = KD + CT
        STEPS = CT * (TAPS + 1)
        ACC0 = N_CH + 2

        def chunk_src(l, c):
            if c < N_IN:
                return w_in[l, c], KD
            if c < N_IN + CT:
                return w_pw[l, c - N_IN], CT
            return w_out[l, c - N_IN - CT], KD

        def rows_of(c):
            return CT if N_IN <= c < N_IN + CT else KD

        def follows(l, c):
            l, c = (l, c) if c < N_CH else (l + 1, c - N_CH)
            return (l, c) if l < DEPTH else None

        TH_SEQ = [("bg", 0), ("bg", 1), ("bg", 2), ("ln", 0), ("ln", 1), ("ln", 2), ("ag", 0), ("ag", 1),
                  ("cg", 0), ("cg", 1), ("cg", 2)]
        TH_L = len(TH_SEQ)
        Y_OF_GATE = {"ag": 0, "bg": 2, "cg": 5}

        def emptied(l, c):
            return ACC0 + N_CH * l + c + 1

        def x_tile(l, k):
            return emptied(l - 1, N_IN + CT + k)

        def bank_of(c):
            return sc[0] if c == 2 else acc[c % 2]

        def v_tile(g):
            return IN_TILES.index(("bv", g) if g < DPAIRS else ("av", g - DPAIRS))

        def rope_of(c):
            kind, j = IN_TILES[c]
            return 2 * j + (kind == "bk") if kind in ("bq", "bk") else None

        def tile_at(n):
            return PRE + n // 2, n % 2 == 1

        block = ctx.enter_context(nc.Block())

        @block.sync
        def _(sp):
            def load(l, c, wait):
                src, k = chunk_src(l, c)
                if wait:
                    sp.wait_ge(lo_ready, N_CH * l + c - RAW + 1)
                sp.dma_start(raw[:, c % RAW, 0:k, :], src).then_inc(raw_in[c % RAW], 16)

            def load_next(l, c):
                if (f := follows(l, c + LOAD_AHEAD)) is not None:
                    load(*f, True)

            def swap(l, r):
                sp.wait_ge(acc_free, emptied(l, IN_TILES.index(("bk" if r % 2 else "bq", r // 2))))
                for h in range(4):
                    o = 32 * (h ^ 1)
                    sp.dma_start(zsw[32 * h:32 * h + 32, :], zs[o:o + 32, :]).then_inc(swap_in, 16)

            def load_bias(l, un):
                b = un - DUNITS
                sp.wait_ge(m_ready, UNITS * l + (un - 1 if b >= 2 else DUNITS - 4))
                sp.dma_start(bias[:, b % 2, :], nabias[l, b]).then_inc(bias_in[b % 2], 16)

            sp.dma_start(par[:, :], prm[0]).then_inc(par_in, 16)
            load(0, 0, False)
            for i, k in enumerate(K_ORDER):
                sp.dma_start(x[:, k, :], xT[:, k, :]).then_inc(x_in[k], 16)
                if i == X_BEFORE_W1 - 1:
                    load(0, 1, False)
            for c in range(2, RAW):
                load(0, c, False)
            sp.dma_start(cs[:, :, :], rope).then_inc(const_in, 16)
            sp.dma_start(cnt[:, :], lncnt).then_inc(const_in, 16)
            sp.dma_start(gf[:, :], gfin).then_inc(const_in, 16)
            for c in range(RAW, LOAD_AHEAD):
                load(0, c, True)
            for l in range(DEPTH):
                for c in range(PRE):
                    load_next(l, c)
                    if (r := rope_of(c)) is not None:
                        swap(l, r)
                for n in range(UNITS):
                    c, ends = tile_at(n)
                    if not ends:
                        load_next(l, c)
                    elif (r := rope_of(c)) is not None:
                        swap(l, r)
                    if n == DUNITS - 4:
                        load_bias(l, DUNITS)
                        load_bias(l, DUNITS + 1)
                    if DUNITS <= n < UNITS - 2:
                        load_bias(l, n + 2)
                for c in range(N_IN, N_CH):
                    load_next(l, c)
                    if c == N_IN + CT and l + 1 < DEPTH:
                        sp.wait_ge(ylo_ready, KD * (l + 1))
                        sp.dma_start(par[:, :], prm[l + 1]).then_inc(par_in, 16)
            for k in range(KD):
                sp.wait_ge(res_ready, k + 1)
                sp.dma_start(out[:, k, :], y[:, k, :]).then_inc(out_in, 16)
            sp.wait_ge(out_in, 16 * KD)

        @block.tensor
        def _(pe):
            def products(c, a_hi, a_lo, first=0, end=None, order=None, ready=None, used=None):
                slot, to, K = c % SPL, bank_of(c), rows_of(c)
                end = K if end is None else end
                for i in range(first, end):
                    k = i if order is None else order[i]
                    if ready is not None:
                        pe.wait_ge(ready[0], ready[1] + i + 1)
                    nc.tensor.matmul(to[:, :], w_hi[:, slot, k, :], a_hi[:, k, :], start=i == 0, stop=False)
                    nc.tensor.matmul(to[:, :], w_lo[:, slot, k, :], a_hi[:, k, :], start=False, stop=False)
                    last = nc.tensor.matmul(to[:, :], w_hi[:, slot, k, :], a_lo[:, k, :], start=False, stop=i == K - 1)
                    if i == K - 1:
                        last.then_inc(tile_done, 1)
                    elif used is not None:
                        last.then_inc(used, 1)

            def open_tile(l, c):
                pe.wait_ge(lo_ready, N_CH * l + c + 1)
                if c == 2:
                    if l:
                        pe.wait_ge(m_ready, UNITS * l)
                else:
                    pe.wait_ge(acc_free, emptied(l, c - 2))

            def in_tile(l, c, first=0, end=KD, ready=None):
                if first == 0:
                    open_tile(l, c)
                products(c, act_hi, act_lo, first, end, order=K_ORDER, ready=ready)

            def take_misc(l, k):
                pe.wait_ge(misc_free, MISC_L * l + k)

            def norm_col(l, k, adds):
                take_misc(l, k)
                pe.wait_ge(add_done, adds)
                for a in range(QT):
                    last = nc.tensor.matmul(misc[:, a * P:(a + 1) * P], ssq[:, a * P:(a + 1) * P], ones[:, :],
                                            start=True, stop=True)
                last.then_inc(misc_ready, 1)

            def norm_bc(l, k, diags):
                take_misc(l, k)
                pe.wait_ge(diag_ready, diags)
                nc.tensor.matmul(misc[:, :], ones[:, :], acc2[:, :],
                                 start=True, stop=True).then_inc(misc_ready, 1)

            def scores(l, n):
                g, h, b = unit(n)
                if n % UPP == 0:
                    if g < DPAIRS:
                        pe.wait_ge(qk_ready, ROPES * l + 2 * g + 2)
                    else:
                        pe.wait_ge(acc_free, emptied(l, IN_TILES.index(("ak", g - DPAIRS))))
                if n >= 2:
                    pe.wait_ge(m_ready, UNITS * l + n - 1)
                q = qpad[:, g % 2, h, b * P:(b + 1) * P]
                if g < DPAIRS:
                    o, k = sc[n % 2][:, :], kT[:, g % 2, :]
                else:
                    o, k = sc[n % 2][:, 0:NKEY], kT[:, g % 2, ROWS * NA_LO[b]:ROWS * NA_LO[b] + NKEY]
                nc.tensor.matmul(o, q, k, start=True, stop=True).then_inc(s_ready, 1)

            def turn(l, n):
                g, h, b = unit(n)
                pe.wait_ge(p_ready, UNITS * l + n + 1)
                if n >= 2:
                    pe.wait_ge(pt_ready, UNITS * l + n - 1)
                blocks = QT if g < DPAIRS else NKEY // P
                for k in range(blocks):
                    last = nc.tensor.transpose(tp[n % 2][:, k * P:(k + 1) * P],
                                               prob[:, n % PROBS, k * P:(k + 1) * P], ident[:, :])
                last.then_inc(t_ready, 1)

            def turn_v(l, g, rnd):
                pe.wait_ge(acc_free, emptied(l, v_tile(g)))
                take_misc(l, MISC_V[g][rnd])
                for i in range(QT):
                    if g < DPAIRS:
                        src = vT[:, i * P:(i + 1) * P]
                    else:
                        b, half = divmod(rnd * QT + i, 2)
                        first = ROWS * NA_LO[b] + half * P
                        src = vT[:, first:first + P]
                    last = nc.tensor.transpose(misc[:, i * P:(i + 1) * P], src, ident[:, :])
                last.then_inc(misc_ready, 1)

            def values(l, g):
                pe.wait_ge(pt_ready, UNITS * l + UPP * (g + 1))
                pe.wait_ge(misc_free, MISC_L * l + MISC_V[g][-1] + 1)
                if g >= 1:
                    pe.wait_ge(pair_final, PAIRS * l + g)
                if g < DPAIRS:
                    for k in range(QT):
                        for h in range(2):
                            last = nc.tensor.matmul(ob[HD * h:HD * (h + 1), :], v[:, g % 2, k, HD * h:HD * (h + 1)],
                                                    pT[:, h, k, :], start=k == 0, stop=k == QT - 1)
                else:
                    for b in range(QT):
                        for half in range(2):
                            for h in range(2):
                                last = nc.tensor.matmul(ob[HD * h:HD * (h + 1), b * P:(b + 1) * P],
                                                        v[:, g % 2, 2 * b + half, HD * h:HD * (h + 1)],
                                                        pT[:, h, half, b * P:(b + 1) * P],
                                                        start=half == 0, stop=half == 1)
                last.then_inc(pv_done, 1)

            def ln_mean(l):
                take_misc(l, MISC_MEAN)
                pe.wait_ge(add_done, ADD_L * l + LN_ADDS)
                nc.tensor.matmul(misc[:, :], mean_w[:, :], ssq[:, :], start=True, stop=True).then_inc(misc_ready, 1)

            pe.wait_ge(consts, 5)
            for l in range(DEPTH):
                in_tile(l, 0, ready=(xlo_ready, KD * l))
                for half in range(2, 2 * PRE):
                    in_tile(l, half // 2, half % 2 * KD // 2, (half % 2 + 1) * KD // 2)
                    if half == (2 if l else 3):
                        norm_col(l, MISC_COL, ADD_L * l + KD - 1)
                    if half == (3 if l else 4):
                        norm_bc(l, MISC_BC, 2 * l + 1)
                for n in range(SLOTS):
                    if n < UNITS:
                        scores(l, n)
                        in_tile(l, tile_at(n)[0], n % 2 * KD // 2, (n % 2 + 1) * KD // 2)
                    else:
                        c = N_IN + n - UNITS
                        open_tile(l, c)
                        pe.wait_ge(slo_ready, CT * (l + 1))
                        products(c, s_hi, s_lo)
                    if n >= UPP + LAG and n % UPP == LAG and n < UNITS + LAG:
                        values(l, n // UPP - 1)
                    if LAG <= n < UNITS + LAG:
                        turn(l, n - LAG)
                    if n == LN_MEAN:
                        ln_mean(l)
                    if n == LN_COL:
                        norm_col(l, MISC_LCOL, ADD_L * (l + 1))
                    if n == LN_BC:
                        norm_bc(l, MISC_LBC, 2 * l + 2)
                    if n in V_AT:
                        turn_v(l, *V_AT[n])
                values(l, PAIRS - 1)
                c = N_IN + CT
                open_tile(l, c)
                products(c, act_hi, act_lo, order=K_ORDER, ready=(ylo_ready, KD * l))
                for c in range(N_IN + CT + 1, N_CH):
                    open_tile(l, c)
                    products(c, act_hi, act_lo, order=K_ORDER, used=act_used if c == N_CH - 1 else None)
            norm_col(DEPTH, 0, ADD_L * DEPTH + KD - 1)
            norm_bc(DEPTH, 1, 2 * DEPTH + 1)

        @block.scalar
        def _(act):
            def split_hi(l, c):
                K = rows_of(c)
                if N_CH * l + c >= SPL:
                    act.wait_ge(tile_done, N_CH * l + c - SPL + 1)
                act.wait_ge(raw_in[c % RAW], 16 * (N_CH // RAW * l + c // RAW + 1))
                nc.scalar.activation(w_hi[:, c % SPL, 0:K, :], raw[:, c % RAW, 0:K, :], ACT.Copy).then_inc(hi_ready, 1)

            def split_next(l, c):
                if (f := follows(l, c + AHEAD)) is not None:
                    split_hi(*f)

            def x_there(l, k):
                if l == 0:
                    act.wait_ge(x_in[k], 16)
                else:
                    act.wait_ge(acc_free, x_tile(l, k))

            def squares(l, i, k):
                x_there(l, k)
                if i >= 2:
                    act.wait_ge(add_done, ADD_L * l + max(1, i - 2))
                nc.scalar.activation(sq[:, i % 2, :], x[:, k, :], ACT.Square).then_inc(sq_ready, 1)

            def ln_squares(l, j):
                act.wait_ge(misc_free, MISC_L * l + MISC_MEAN + 1)
                if j >= 2:
                    act.wait_ge(add_done, ADD_L * l + LN_ADDS + 1)
                nc.scalar.activation(sq[:, j % 2, :], y[:, KD - CT + j, :], ACT.Square).then_inc(sq_ready, 1)

            def x_hi(l, i):
                k = K_ORDER[i]
                x_there(l, k)
                if l:
                    if i < KD - 1:
                        act.wait_ge(act_used, (KD - 1) * (l - 1) + i + 1)
                    else:
                        act.wait_ge(tile_done, N_CH * l)
                nc.scalar.activation(act_hi[:, k, :], x[:, k, :], ACT.Copy,
                                     scale=par[:, P_G + k:P_G + k + 1]).then_inc(xhi_ready, 1)

            def tanh(l, key, src):
                i = TH_SEQ.index(key)
                act.wait_ge(th_used, TH_L * l + i)
                nc.scalar.activation(th[:, :], src, ACT.Tanh).then_inc(th_ready, 1)

            def exps(l, n):
                w = SEQ if n < DUNITS else NKEY
                act.wait_ge(m_ready, UNITS * l + n + 1)
                nc.scalar.activation(prob[:, n % PROBS, 0:w], prob[:, n % PROBS, 0:w], ACT.Exp, scale=-1.0,
                                     bias=nmx[:, n % 4:n % 4 + 1],
                                     accum_out=den[:, n % 4:n % 4 + 1]).then_inc(e_ready, 1)

            def empty_turn(l, n):
                g, h, b = unit(n)
                act.wait_ge(t_ready, UNITS * l + n + 1)
                if n % UPP == 0 and g:
                    act.wait_ge(pv_done, PAIRS * l + g)
                kk = QT if g < DPAIRS else NKEY // P
                nc.scalar.activation(pT[:, h, 0:kk, b * P:(b + 1) * P],
                                     tp[n % 2][:, 0:kk * P].rearrange("p (k t) -> p k t", t=P),
                                     ACT.Copy).then_inc(pt_ready, 1)

            def y_hi(l, i):
                k = K_ORDER[i]
                if i == 0:
                    act.wait_ge(tile_done, N_CH * l + N_IN)
                if k >= KD - CT:
                    act.wait_ge(acc_free, emptied(l, N_IN + k - (KD - CT)))
                else:
                    act.wait_ge(pair_final, PAIRS * l + Y_OF_PAIR.index(k) + 1)
                nc.scalar.activation(act_hi[:, k, :], y[:, k, :], ACT.Copy).then_inc(yhi_ready, 1)

            def v_out(l, g, rnd):
                if g >= 2:
                    act.wait_ge(pv_done, PAIRS * l + g - 1)
                act.wait_ge(misc_ready, MISC_L * l + MISC_V[g][rnd] + 1)
                nc.scalar.activation(v[:, g % 2, rnd * QT:(rnd + 1) * QT, :],
                                     misc[:, :].rearrange("p (k t) -> p k t", t=P), ACT.Copy).then_inc(misc_free, 1)

            split_hi(0, 0)
            for l in range(DEPTH):
                act.wait_ge(par_in, 16 * (l + 1))
                for i in range(KD - 1):
                    x_hi(l, i)
                    if l == 0 and i == X_BEFORE_W1 - 1:
                        squares(0, 0, K_ORDER[0])
                        squares(0, 1, K_ORDER[1])
                if l == 0:
                    x_hi(l, KD - 1)
                    split_hi(0, 1)
                    for i in range(2, KD):
                        squares(0, i, K_ORDER[i])
                        if i == KD // 2:
                            split_hi(0, 2)
                else:
                    squares(l, KD - 1, KD - 1)
                    x_hi(l, KD - 1)
                for c in range(PRE):
                    split_next(l, c)
                    kind, j = IN_TILES[c]
                    if kind == "cb":
                        mid = u[:, j, HALO:HALO + SEQ]
                        act.wait_ge(acc_free, emptied(l, c))
                        nc.scalar.activation(mid, mid, ACT.Tanh).then_inc(cbt_ready, 1)
                for n in range(SLOTS):
                    if n > LAG:
                        empty_turn(l, n - LAG - 1)
                    if n < UNITS:
                        exps(l, n)
                        if n % 2 == 0:
                            split_next(l, tile_at(n)[0])
                    else:
                        split_next(l, N_IN + n - UNITS)
                    if n - 1 in V_AT:
                        v_out(l, *V_AT[n - 1])
                    if n == LN_MEAN + 1:
                        for j in range(CT):
                            ln_squares(l, j)
                    if 0 < n - LN_SILU <= CT:
                        j = n - LN_SILU - 1
                        act.wait_ge(th_used, TH_L * l + TH_SEQ.index(("ln", j)) + 1)
                        nc.scalar.activation(s_hi[:, j, :], y[:, KD - CT + j, :], ACT.Copy).then_inc(shi_ready, 1)
                    if 0 <= n - LN_SILU < CT:
                        j = n - LN_SILU
                        act.wait_ge(hn_ready, CT * (l + 1))
                        tanh(l, ("ln", j), y[:, KD - CT + j, :])
                    if n and n % 2 == 0 and n <= UNITS:
                        c = tile_at(n - 1)[0]
                        kind, j = IN_TILES[c]
                        if kind in Y_OF_GATE:
                            act.wait_ge(acc_free, emptied(l, c))
                            tanh(l, (kind, j), y[:, Y_OF_GATE[kind] + j, :])
                    if n >= UNITS:
                        y_hi(l, n - UNITS)
                for i in range(SLOTS - UNITS, KD):
                    y_hi(l, i)
                for c in range(N_IN + CT, N_CH):
                    split_next(l, c)
                    if c > N_IN + CT:
                        k = c - (N_IN + CT) - 1
                        squares(l + 1, k, k)
            squares(DEPTH, KD - 1, KD - 1)

        @block.gpsimd
        def _(pool):
            def split_lo(l, c):
                K = rows_of(c)
                pool.wait_ge(hi_ready, N_CH * l + c + 1)
                nc.gpsimd.tensor_tensor(w_lo[:, c % SPL, 0:K, :], raw[:, c % RAW, 0:K, :],
                                        w_hi[:, c % SPL, 0:K, :], ALU.subtract).then_inc(lo_ready, 1)

            def split_next(l, c):
                if (f := follows(l, c + AHEAD)) is not None:
                    split_lo(*f)

            def add_squares(l, k, base=0):
                sqs, adds = (SQ_L * l, ADD_L * l) if base == 0 else (SQ_L * l + KD, ADD_L * l + LN_ADDS)
                pool.wait_ge(sq_ready, sqs + k + 1)
                if k >= 2:
                    pool.wait_ge(add_done, adds + k - 1)
                a = sq[:, 0, :] if k == 1 else ssq[:, :]
                nc.gpsimd.tensor_tensor(ssq[:, :], a, sq[:, k % 2, :], ALU.add).then_inc(add_done, 1)

            def root(l, k):
                pool.wait_ge(misc_free, MISC_L * l + k + 1)
                nc.gpsimd.tensor_tensor(rcol[:, :], col[:, :], nhalf[:, :], ALU.pow).then_inc(pow_ready, 1)

            def norm(l, n):
                w = SEQ if n < DUNITS else NKEY
                pool.wait_ge(r_ready, UNITS * l + n + 1)
                nc.gpsimd.tensor_scalar(prob[:, n % PROBS, 0:w], prob[:, n % PROBS, 0:w], rden[:, n % 4:n % 4 + 1],
                                        1.0, ALU.mult, ALU.mult).then_inc(p_ready, 1)

            def rotate(l, r):
                pool.wait_ge(swap_in, 64 * (ROPES * l + r + 1))
                nc.gpsimd.tensor_tensor(zsw[:, :], zsw[:, :], cs[:, 1, :], ALU.mult).then_inc(t2_ready, 1)

            nc.gpsimd.memset(ident[:, :], 0.0).then_inc(consts, 1)
            nc.gpsimd.memset(ones[:, :], 1.0).then_inc(consts, 1)
            nc.gpsimd.memset(mean_w[:, :], 1.0 / CONV_CH).then_inc(consts, 1)
            nc.gpsimd.memset(nhalf[:, :], -0.5).then_inc(consts, 1)
            pool.wait_ge(consts, 4)
            nc.gpsimd.affine_select(out=ident[:, :], in_=ident[:, :], compare_op=ALU.not_equal, fill=1.0, base=0,
                                    pattern=[[-1, P]], channel_multiplier=1).then_inc(consts, 1)
            pool.wait_ge(lo_ready, 1)
            split_lo(0, 1)
            for l in range(DEPTH):
                if l == 0:
                    split_lo(0, 2)
                    pool.wait_ge(const_in, 48)
                else:
                    add_squares(l, KD - 1)
                root(l, MISC_COL)
                for c in range(PRE):
                    split_next(l, c)
                    if c < PRE - 1 and (r := rope_of(c)) is not None:
                        rotate(l, r)
                for n in range(UNITS + 1):
                    if n:
                        norm(l, n - 1)
                    if n < UNITS and n % 2 == 0:
                        split_next(l, tile_at(n)[0])
                    if n % 2 and (r := rope_of(tile_at(n - 2)[0])) is not None:
                        rotate(l, r)
                    if n == LN_SUM:
                        pool.wait_ge(conv_step, STEPS * (l + 1))
                        for j in range(1, CT):
                            a = y[:, KD - CT, :] if j == 1 else ssq[:, :]
                            nc.gpsimd.tensor_tensor(ssq[:, :], a, y[:, KD - CT + j, :], ALU.add).then_inc(add_done, 1)
                            pool.wait_ge(add_done, ADD_L * l + KD - 1 + j)
                    if n == LN_MEAN + 1:
                        for j in range(1, CT):
                            add_squares(l, j, base=1)
                    if n == LN_BC - 1:
                        root(l, MISC_LCOL)
                for c in range(N_IN, N_CH):
                    split_next(l, c)
                    if c >= N_IN + CT + 2:
                        add_squares(l + 1, c - (N_IN + CT) - 1)
            add_squares(DEPTH, KD - 1)
            root(DEPTH, MISC_COL)

        @block.vector
        def _(dve):
            own = [0]

            def step(ins):
                own[0] += 1
                ins.then_inc(dve_own, 1)
                dve.wait_ge(dve_own, own[0])

            def column(l, k, width):
                dve.wait_ge(misc_ready, MISC_L * l + k + 1)
                nc.vector.tensor_scalar(col[:, :], misc[:, :].rearrange("p (a t) -> p a t", a=QT)[:, :, 0], 1.0 / width, EPS, ALU.mult, ALU.add)\
                    .then_inc(misc_free, 1)

            def diagonals(i):
                dve.wait_ge(pow_ready, i + 1)
                for a in range(QT):
                    last = nc.vector.tensor_scalar(diag[:, a, :], ident[:, :], rcol[:, a:a + 1], None, ALU.mult)
                last.then_inc(diag_ready, 1)

            def take_factor(l):
                dve.wait_ge(misc_ready, MISC_L * l + MISC_BC + 1)
                nc.vector.tensor_copy(rstd[:, :], misc[:, :]).then_inc(misc_free, 1)
                dve.wait_ge(misc_free, MISC_L * l + MISC_BC + 1)

            def scaled(dst, c, factor):
                return nc.vector.scalar_tensor_tensor(out=dst, in0=bank_of(c)[:, :], scalar=factor, in1=rstd[:, :],
                                                      op0=ALU.mult, op1=ALU.mult)

            def scaled_by_column(dst, c, factor):
                def view(a):
                    return a.rearrange("p (r c) -> p r c", c=GRID_W)
                return nc.vector.scalar_tensor_tensor(out=dst.rearrange("p (c r) -> p r c", c=GRID_W),
                                                      in0=view(bank_of(c)[:, :]), scalar=factor, in1=view(rstd[:, :]),
                                                      op0=ALU.mult, op1=ALU.mult)

            def empty_tile(l, c):
                kind, j = IN_TILES[c]
                dve.wait_ge(tile_done, N_CH * l + c + 1)
                if kind == "cb":
                    scaled(u[:, j, HALO:HALO + SEQ], c, 0.5).then_inc(acc_free, 1)
                elif kind == "ca":
                    half = y[:, KD - CT + j, :]
                    scaled(half, c, 0.5).then_inc(acc_free, 1)
                    dve.wait_ge(acc_free, emptied(l, c))
                    dve.wait_ge(cbt_ready, CT * l + j + 1)
                    mid = u[:, j, HALO:HALO + SEQ]
                    nc.vector.scalar_tensor_tensor(out=mid, in0=mid, scalar=1.0, in1=half, op0=ALU.add,
                                                   op1=ALU.mult).then_inc(u_ready, 1)
                elif kind in ("bq", "bk"):
                    scaled(zs[:, :], c, HD ** -0.5 if kind == "bq" else 1.0).then_inc(acc_free, 1)
                    dve.wait_ge(acc_free, emptied(l, c))
                    nc.vector.tensor_tensor(zc[:, :], zs[:, :], cs[:, 0, :], ALU.mult).then_inc(dve_own, 1)
                    own[0] += 1
                elif kind in ("bv", "av"):
                    g = j if kind == "bv" else DPAIRS + j
                    if g:
                        dve.wait_ge(misc_free, MISC_L * l + MISC_V[g - 1][-1] + 1)
                    (scaled if kind == "bv" else scaled_by_column)(vT[:, :], c, 1.0).then_inc(acc_free, 1)
                elif kind == "aq":
                    g = DPAIRS + j
                    for h in range(2):
                        o = HD * h
                        dst = qpad[o:o + HD, g % 2, h, :].rearrange("p (b r c) -> p r b c", b=QT, r=ROWS)
                        src = bank_of(c)[o:o + HD, :].rearrange("p (r b c) -> p r b c", b=QT, r=ROWS)
                        fac = rstd[o:o + HD, :].rearrange("p (r b c) -> p r b c", b=QT, r=ROWS)
                        last = nc.vector.tensor_tensor(dst, src, fac, ALU.mult)
                    last.then_inc(acc_free, 1)
                elif kind == "ak":
                    scaled_by_column(kT[:, (DPAIRS + j) % 2, :], c, HD ** -0.5).then_inc(acc_free, 1)
                else:
                    scaled(y[:, Y_OF_GATE[kind] + j, :], c, 0.5).then_inc(acc_free, 1)

            def rotated(l, r):
                g = r // 2
                dve.wait_ge(t2_ready, ROPES * l + r + 1)
                dve.wait_ge(dve_own, own[0])
                if r % 2:
                    last = nc.vector.tensor_tensor(kT[:, g % 2, :], zc[:, :], zsw[:, :], ALU.add)
                else:
                    for h in range(2):
                        o = HD * h
                        last = nc.vector.tensor_tensor(qpad[o:o + HD, g % 2, h, :], zc[o:o + HD, :],
                                                       zsw[o:o + HD, :], ALU.add)
                last.then_inc(qk_ready, 1)

            def conv_taps(l, first, count):
                for i in range(first, min(first + count, STEPS)):
                    j, t = divmod(i, TAPS + 1)
                    dst = (y[:, KD - CT + j, :], acc2[:, :])[t % 2]
                    if t == 0:
                        dve.wait_ge(u_ready, CT * l + j + 1)
                    if STEPS * l + i:
                        dve.wait_ge(conv_step, STEPS * l + (i if t == TAPS or t < 2 else i - 1))
                    src = u[:, j, t % TAPS:t % TAPS + SEQ]
                    w = par[:, P_W + TAPS * j + t % TAPS:P_W + TAPS * j + t % TAPS + 1]
                    if t == 0:
                        ins = nc.vector.tensor_scalar(dst, src, w, par[:, P_B + j:P_B + j + 1], ALU.mult, ALU.add)
                    elif t == 1:
                        ins = nc.vector.tensor_scalar(dst, src, w, None, ALU.mult)
                    elif t < TAPS:
                        ins = nc.vector.scalar_tensor_tensor(out=dst, in0=src, scalar=w, in1=dst, op0=ALU.mult,
                                                             op1=ALU.add)
                    else:
                        a = y[:, KD - CT + j, :]
                        ins = nc.vector.tensor_tensor(a, a, acc2[:, :], ALU.add)
                    ins.then_inc(conv_step, 1)

            def maxima(l, n):
                g, h, b = unit(n)
                dve.wait_ge(s_ready, UNITS * l + n + 1)
                if n >= PROBS:
                    dve.wait_ge(t_ready, UNITS * l + n - PROBS + 1)
                if g < DPAIRS:
                    w, add = SEQ, cnt[:, P * (QT - 1 - b):P * (QT - 1 - b) + SEQ]
                else:
                    w, i = NKEY, n - DUNITS
                    dve.wait_ge(bias_in[i % 2], 16 * (UPP * l + i // 2 + 1))
                    add = bias[:, i % 2, :]
                nc.vector.tensor_tensor_reduce(out=prob[:, n % PROBS, 0:w], in0=sc[n % 2][:, 0:w], in1=add, scale=-1.0,
                                               scalar=3e38, op0=ALU.add, op1=ALU.min,
                                               accum_out=nmx[:, n % 4:n % 4 + 1]).then_inc(m_ready, 1)

            def reciprocal(l, n):
                dve.wait_ge(e_ready, UNITS * l + n + 1)
                nc.vector.reciprocal(rden[:, n % 4:n % 4 + 1], den[:, n % 4:n % 4 + 1]).then_inc(r_ready, 1)

            def silu(l, key, t):
                dve.wait_ge(th_ready, TH_L * l + TH_SEQ.index(key) + 1)
                nc.vector.scalar_tensor_tensor(out=t, in0=th[:, :], scalar=1.0, in1=t, op0=ALU.add,
                                               op1=ALU.mult).then_inc(th_used, 1)

            def gated(l, g):
                dve.wait_ge(pv_done, PAIRS * l + g + 1)
                gate = ("bg", g) if g < DPAIRS else ("ag", g - DPAIRS)
                dve.wait_ge(th_used, TH_L * l + TH_SEQ.index(gate) + 1)
                t = y[:, Y_OF_PAIR[g], :]
                if g < DPAIRS:
                    ins = nc.vector.tensor_tensor(t, ob[:, :], t, ALU.mult)
                else:
                    t = t.rearrange("p (r b c) -> p r b c", b=QT, r=ROWS)
                    o = ob[:, :].rearrange("p (b r c) -> p r b c", b=QT, r=ROWS)
                    ins = nc.vector.tensor_tensor(t, o, t, ALU.mult)
                ins.then_inc(pair_final, 1)

            def pointwise(l, j):
                dve.wait_ge(tile_done, N_CH * l + N_IN + j + 1)
                dve.wait_ge(th_used, TH_L * l + TH_SEQ.index(("cg", j)) + 1)
                t = y[:, KD - CT + j, :]
                nc.vector.scalar_tensor_tensor(out=t, in0=acc[(N_IN + j) % 2][:, :],
                                               scalar=par[:, P_PB + j:P_PB + j + 1], in1=t, op0=ALU.add,
                                               op1=ALU.mult).then_inc(acc_free, 1)

            def y_lo(l, i):
                k = K_ORDER[i]
                dve.wait_ge(yhi_ready, KD * l + i + 1)
                nc.vector.tensor_tensor(act_lo[:, k, :], y[:, k, :], act_hi[:, k, :], ALU.subtract)\
                    .then_inc(ylo_ready, 1)

            def add_product(l, k):
                c = N_IN + CT + k
                dve.wait_ge(tile_done, N_CH * l + c + 1)
                nc.vector.tensor_tensor(x[:, k, :], x[:, k, :], bank_of(c)[:, :], ALU.add).then_inc(acc_free, 1)

            def first_add(i):
                dve.wait_ge(sq_ready, i + 1)
                if i >= 2:
                    dve.wait_ge(add_done, i - 1)
                nc.vector.tensor_tensor(ssq[:, :], sq[:, 0, :] if i == 1 else ssq[:, :], sq[:, i % 2, :],
                                        ALU.add).then_inc(add_done, 1)

            def x_lo(l, i):
                k = K_ORDER[i]
                dve.wait_ge(xhi_ready, KD * l + i + 1)
                nc.vector.scalar_tensor_tensor(out=act_lo[:, k, :], in0=x[:, k, :],
                                               scalar=par[:, P_G + k:P_G + k + 1], in1=act_hi[:, k, :],
                                               op0=ALU.mult, op1=ALU.subtract).then_inc(xlo_ready, 1)

            nc.vector.memset(u[:, :, :], 0.0).then_inc(cleared, 1)
            nc.vector.memset(qpad[:, :, :, :], 0.0).then_inc(cleared, 1)
            dve.wait_ge(cleared, 2)
            nc.vector.memset(nmx[:, :], 0.0).then_inc(acc_free, ACC0)
            for l in range(DEPTH):
                dve.wait_ge(par_in, 16 * (l + 1))
                step(nc.vector.tensor_scalar(parh[:, :], par[:, P_LG:P_LG + 2 * CT], 0.5, None, ALU.mult))
                if l == 0:
                    dve.wait_ge(hi_ready, 1)
                    nc.vector.tensor_tensor(w_lo[:, 0, :, :], raw[:, 0, :, :], w_hi[:, 0, :, :],
                                            ALU.subtract).then_inc(lo_ready, 1)
                for i in range(KD):
                    if l and i == X_LATE:
                        add_product(l - 1, KD - 1)
                    x_lo(l, i)
                    if l == 0 and i == X_BEFORE_W1 - 1:
                        first_add(1)
                if l == 0:
                    for i in range(2, KD):
                        first_add(i)
                column(l, MISC_COL, D)
                if l == 0:
                    dve.wait_ge(consts, 5)
                    dve.wait_ge(const_in, 48)
                diagonals(2 * l)
                take_factor(l)
                taps = 0
                for c in range(PRE):
                    empty_tile(l, c)
                    if c >= 1:
                        conv_taps(l, taps, PRE_TAPS)
                        taps += PRE_TAPS
                    if c and (r := rope_of(c - 1)) is not None:
                        rotated(l, r)
                for n in range(SLOTS):
                    if n < UNITS:
                        maxima(l, n)
                    if 0 < n <= UNITS:
                        reciprocal(l, n - 1)
                    if n > UPP + LAG and n % UPP == LAG + 1 and n < SLOTS - 1:
                        gated(l, n // UPP - 1)
                    if n and n % 2 == 1:
                        c = tile_at(n - 2)[0] if 2 <= n <= UNITS + 1 else 0
                        if n >= 2 and IN_TILES[c][0] in Y_OF_GATE:
                            kind, j = IN_TILES[c]
                            silu(l, (kind, j), y[:, Y_OF_GATE[kind] + j, :])
                    if n and n % 2 == 0 and n <= UNITS:
                        if (r := rope_of(tile_at(n - 4)[0])) is not None:
                            rotated(l, r)
                        empty_tile(l, tile_at(n - 1)[0])
                    conv_taps(l, taps, SLOT_TAPS)
                    taps += SLOT_TAPS
                    if n == LN_MEAN:
                        dve.wait_ge(misc_ready, MISC_L * l + MISC_MEAN + 1)
                        for j in range(CT):
                            t = y[:, KD - CT + j, :]
                            last = nc.vector.tensor_tensor(t, t, misc[:, :], ALU.subtract)
                        last.then_inc(misc_free, 1)
                    if n == LN_COL:
                        column(l, MISC_LCOL, CONV_CH)
                    if n == LN_BC - 1:
                        diagonals(2 * l + 1)
                    if n == LN_BC:
                        dve.wait_ge(misc_ready, MISC_L * l + MISC_LBC + 1)
                        for j in range(CT):
                            t = y[:, KD - CT + j, :]
                            last = nc.vector.tensor_tensor(t, t, misc[:, :], ALU.mult)
                        last.then_inc(misc_free, 1)
                        dve.wait_ge(misc_free, MISC_L * l + MISC_LBC + 1)
                        for j in range(CT):
                            t = y[:, KD - CT + j, :]
                            nc.vector.tensor_scalar(t, t, parh[:, j:j + 1], parh[:, CT + j:CT + j + 1], ALU.mult,
                                                    ALU.add).then_inc(hn_ready, 1)
                    if 0 <= n - LN_SILU < CT:
                        j = n - LN_SILU
                        silu(l, ("ln", j), y[:, KD - CT + j, :])
                    if 0 < n - LN_SILU <= CT:
                        j = n - LN_SILU - 1
                        dve.wait_ge(shi_ready, CT * l + j + 1)
                        nc.vector.tensor_tensor(s_lo[:, j, :], y[:, KD - CT + j, :], s_hi[:, j, :], ALU.subtract)\
                            .then_inc(slo_ready, 1)
                    if n > UNITS:
                        pointwise(l, n - UNITS - 1)
                        y_lo(l, n - UNITS - 1)
                pointwise(l, CT - 1)
                gated(l, PAIRS - 1)
                for i in range(CT - 1, KD):
                    y_lo(l, i)
                for k in range(KD - 1):
                    add_product(l, k)
            add_product(DEPTH - 1, KD - 1)
            column(DEPTH, MISC_COL, D)
            diagonals(2 * DEPTH)
            take_factor(DEPTH)
            for k in range(KD):
                nc.vector.scalar_tensor_tensor(out=y[:, k, :], in0=x[:, k, :], scalar=gf[:, k:k + 1],
                                               in1=rstd[:, :], op0=ALU.mult, op1=ALU.mult).then_inc(res_ready, 1)


def by_partition(a):
    *lead, r, c = a.shape
    a = a.reshape(*lead, r // P, P, c // P, P)
    n = len(lead)
    return a.transpose(*range(n), n + 2, n + 1, n, n + 3)


def dil_table():
    diff = np.arange(NEG_TILE)[None, :] - P * (QT - 1) - np.arange(P)[:, None]
    count = np.zeros(diff.shape, np.int64)
    for w, d in PATTERNS:
        count += (np.abs(diff) <= (w // 2) // d * d) & (diff % d == 0)
    return np.where(count > 0, np.log(np.maximum(count, 1)), NEG).astype(np.float32)


def rope_table():
    half = HD // 2
    ang = np.arange(SEQ)[None, :] * 10000.0 ** (-np.arange(half) * 2.0 / HD)[:, None]
    cos, sin = np.cos(ang), np.sin(ang)
    out = np.stack([np.tile(cos, (4, 1)), np.concatenate([-sin, sin, -sin, sin])], 1)
    return np.ascontiguousarray(out.astype(np.float32))


def na_bias(rpb):
    b, r, c = np.meshgrid(np.arange(QT), np.arange(ROWS), np.arange(GRID_W // QT), indexing="ij")
    col = (GRID_W // QT * b + c).reshape(QT, P)
    row = r.reshape(QT, P)
    j, i = np.meshgrid(np.arange(NAW), np.arange(ROWS), indexing="ij")
    i, j = i.ravel(), j.ravel()
    key_col = np.array(NA_LO)[:, None] + j[None, :]
    first = np.clip(col - WIN_COLS // 2, 0, GRID_W - WIN_COLS)
    inside = (key_col[:, None, :] >= first[:, :, None]) & (key_col[:, None, :] < first[:, :, None] + WIN_COLS)
    at_r = i[None, None, :] - row[:, :, None] + ROWS - 1
    at_c = np.clip(key_col[:, None, :] - col[:, :, None] + WIN_COLS - 1, 0, 2 * WIN_COLS - 2)
    full = np.where(inside, rpb[:, :, at_r, at_c], np.float32(NEG))
    L = rpb.shape[0]
    full = full.reshape(L, NA_HEADS // 2, 2, QT, P, NKEY).transpose(0, 1, 3, 2, 4, 5)
    return np.ascontiguousarray(full.reshape(L, 2 * UPP, P, NKEY))


def kernel(x, norm_g, w_in, na_rpb, conv_w, conv_b, conv_ln_g, conv_ln_b, pw_w, pw_b, w_out, final_g):
    import concourse.bacc as bacc
    from concourse.bass_utils import run_bass_kernel_spmd

    x, norm_g, w_in, na_rpb, conv_w, conv_b, conv_ln_g, conv_ln_b, pw_w, pw_b, w_out, final_g = map(
        np.asarray, (x, norm_g, w_in, na_rpb, conv_w, conv_b, conv_ln_g, conv_ln_b, pw_w, pw_b, w_out, final_g))

    def tiles(a):
        return a.reshape(DEPTH, -1, P).transpose(0, 2, 1)

    order = [PART_AT[kind] // P + j for kind, j in IN_TILES]
    taps = conv_w.transpose(0, 2, 1).reshape(DEPTH, CT, P, TAPS).transpose(0, 2, 1, 3).reshape(DEPTH, P, CT * TAPS)
    arrays = {
        "xT": x[0].T.reshape(KD, P, SEQ).transpose(1, 0, 2),
        "w_in": by_partition(w_in)[:, order],
        "w_pw": by_partition(pw_w),
        "w_out": by_partition(w_out),
        "prm": np.concatenate([tiles(norm_g), taps, tiles(conv_b), tiles(conv_ln_g), tiles(conv_ln_b), tiles(pw_b)], 2),
        "gfin": final_g.reshape(KD, P).T,
        "nabias": na_bias(na_rpb),
        "lncnt": dil_table(),
        "rope": rope_table(),
    }
    arrays = {k: np.ascontiguousarray(a) for k, a in arrays.items()}
    nc = bacc.Bacc("TRN2", target_bir_lowering=False, num_devices=1)
    aps = [nc.dram_tensor(k, a.shape, mybir.dt.from_np(a.dtype), kind="ExternalInput").ap() for k, a in arrays.items()]
    aps.append(nc.dram_tensor("out", (P, KD, SEQ), F32, kind="ExternalOutput").ap())
    build(nc, *aps)
    got = run_bass_kernel_spmd(nc, [arrays], core_ids=[0]).results[0]["out"]
    return got.transpose(1, 0, 2).reshape(D, SEQ).T.reshape(1, SEQ, D)
```

```python
from contextlib import ExitStack

import numpy as np
import concourse.bass as bass
from concourse import mybir

F32 = mybir.dt.float32
F32R = mybir.dt.float32r
ALU = mybir.AluOpType
ACT = mybir.ActivationFunctionType

P = 128
SEQ = 512
D = 1024
DEPTH = 2
GRID_W = 64
ROWS = SEQ // GRID_W
HD = 64
NA_HEADS, DIL_HEADS = 4, 6
WIN_COLS = 16
PATTERNS = ((128, 1), (512, 4), (2048, 16))
CONV_CH = 384
TAPS = 31
HALO = TAPS // 2
EPS = 1e-6
NEG = -1e30
KD = D // P
CT = CONV_CH // P
QT = SEQ // P

IN_TILES = [("cb", 0), ("bq", 0), ("ca", 0), ("bk", 0), ("cb", 1), ("ca", 1), ("bq", 1), ("cb", 2), ("bk", 1),
            ("ca", 2), ("bv", 0), ("bq", 2), ("bg", 0),
            ("bk", 2), ("bv", 1), ("bg", 1), ("bv", 2),
            ("aq", 0), ("ak", 0), ("av", 0), ("bg", 2),
            ("aq", 1), ("ak", 1), ("av", 1), ("ag", 0),
            ("ag", 1), ("cg", 0), ("cg", 1), ("cg", 2)]
PART_AT = {"aq": 0, "ak": 256, "av": 512, "ag": 768, "bq": 1024, "bk": 1408, "bv": 1792, "bg": 2176,
           "ca": 2560, "cb": 2944, "cg": 3328}
N_IN = len(IN_TILES)
PRE = 9
N_CH = N_IN + CT + KD
RAW = 2
SPL = 4
AHEAD = SPL - 1
LOAD_AHEAD = AHEAD + RAW
assert N_CH % RAW == 0 and N_CH % SPL == 0

PAIRS = 5
DPAIRS = DIL_HEADS // 2
UPP = 8
UNITS = PAIRS * UPP
LAG = 2
PROBS = LAG + 2
SLOTS = UNITS + LAG + 1
DUNITS = DPAIRS * UPP
Y_OF_PAIR = [2, 3, 4, 0, 1]
K_ORDER = [2, 3, 4, 0, 5, 6, 1, 7]
NAW = 32
NA_LO = [0, 8, 24, 32]
NKEY = ROWS * NAW
NEG_TILE = 896
PREP = 8 + CT * TAPS + 4 * CT
P_G, P_W, P_B = 0, 8, 8 + CT * TAPS
P_LG, P_LB, P_PB = P_B + CT, P_B + 2 * CT, P_B + 3 * CT

W0_FIRST = max(K_ORDER[:KD // 2]) + 1
X_BEFORE_W1 = 6
POOL_SQ = 4
WARM = 13
COL_HALF, BC_HALF = 2, 3
X_LATE = 6

LN_SUM, LN_MEAN, LN_COL, LN_BC, LN_SILU = 23, 24, 27, 30, 31


def taps_in(c=None, n=None):
    if c is not None:
        if c < IN_TILES.index(("ca", 0)):
            return 0
        return 4 if c < PRE - 1 else 2
    if n in (0, 4):
        return 2
    return 3 if n < 12 else 4


def unit(n):
    return n // UPP, n % 2, (n % UPP) // 2


def build(nc, xT, w_in, w_pw, w_out, prm, gfin, nabias, lncnt, rope, out):
    with ExitStack() as ctx:
        def sb(name, shape, dt=F32):
            return ctx.enter_context(nc.sbuf_tensor(name, shape, dt))

        def bank(name):
            return ctx.enter_context(nc.psum_tensor(name, [P, SEQ], F32))

        def sem(name):
            return ctx.enter_context(nc.semaphore(name))

        x = sb("x", [P, KD, SEQ])
        act_hi = sb("act_hi", [P, KD, SEQ], F32R)
        act_lo = sb("act_lo", [P, KD, SEQ], F32R)
        y = sb("y", [P, KD, SEQ])
        raw = sb("raw", [P, RAW, KD, P])
        w_hi = sb("w_hi", [P, SPL, KD, P], F32R)
        w_lo = sb("w_lo", [P, SPL, KD, P], F32R)
        qs = sb("qs", [P, 2, 2, SEQ], F32R)
        k_hi = sb("k_hi", [P, 2, 2, SEQ], F32R)
        k_lo = sb("k_lo", [P, 2, 2, SEQ], F32R)
        v = sb("v", [P, 2, 2 * QT, P])
        vT = sb("vT", [P, SEQ])
        zc = sb("zc", [P, SEQ])
        u = sb("u", [P, CT, SEQ + 2 * HALO])
        acc2 = sb("acc2", [P, SEQ])
        s_hi = sb("s_hi", [P, CT, SEQ], F32R)
        s_lo = sb("s_lo", [P, CT, SEQ], F32R)
        th = sb("th", [P, SEQ])
        prob = sb("prob", [P, PROBS, SEQ])
        pT = sb("pT", [P, 2, QT, SEQ])
        bias = sb("bias", [P, 2, NKEY])
        sq = sb("sq", [P, 2, SEQ])
        zs, zsw = sq[:, 0, :], sq[:, 1, :]
        ssq = sb("ssq", [P, SEQ])
        rstd = sb("rstd", [P, SEQ])
        diag = acc2[:, :].rearrange("p (a t) -> p a t", a=QT)
        cnt = sb("cnt", [P, NEG_TILE])
        cs = sb("cs", [P, 2, SEQ])
        ident = sb("ident", [P, P])
        ones = sb("ones", [P, P])
        mean_w = sb("mean_w", [P, P])
        par = sb("par", [P, PREP])
        parh = sb("parh", [P, 2 * CT])
        gf = sb("gf", [P, KD])
        nmx = sb("nmx", [P, 4])
        den = sb("den", [P, 4])
        rden = sb("rden", [P, 4])
        col = sb("col", [P, QT])
        rcol = sb("rcol", [P, QT])
        nhalf = sb("nhalf", [P, QT])

        acc = [bank("acc0"), bank("acc1")]
        sc = [bank("sc0"), bank("sc1")]
        tp = [bank("tp0"), bank("tp1")]
        ob = bank("ob")
        misc = bank("misc")

        raw_in = [sem(f"raw_in{i}") for i in range(RAW)]
        x_in = [sem(f"x_in{k}") for k in range(KD)]
        const_in = sem("const_in")
        par_in = sem("par_in")
        bias_in = [sem(f"bias_in{i}") for i in range(2)]
        swap_in = sem("swap_in")
        out_in = sem("out_in")
        consts = sem("consts")
        cleared = sem("cleared")
        hi_ready = sem("hi_ready")
        lo_ready = sem("lo_ready")
        w0_hi = sem("w0_hi")
        w0_lo = sem("w0_lo")
        xhi_ready = sem("xhi_ready")
        xlo_ready = sem("xlo_ready")
        yhi_ready = sem("yhi_ready")
        ylo_ready = sem("ylo_ready")
        tile_done = sem("tile_done")
        act_used = sem("act_used")
        acc_free = sem("acc_free")
        sq_ready = sem("sq_ready")
        pool_sq = sem("pool_sq")
        add_done = sem("add_done")
        misc_ready = sem("misc_ready")
        misc_free = sem("misc_free")
        pow_ready = sem("pow_ready")
        diag_ready = sem("diag_ready")
        cbt_ready = sem("cbt_ready")
        u_ready = sem("u_ready")
        conv_step = sem("conv_step")
        t2_ready = sem("t2_ready")
        zc_ready = sem("zc_ready")
        qk_hi = sem("qk_hi")
        q_lo = sem("q_lo")
        klo_own = sem("klo_own")
        klo_other = sem("klo_other")
        s_ready = sem("s_ready")
        m_ready = sem("m_ready")
        e_ready = sem("e_ready")
        r_ready = sem("r_ready")
        p_ready = sem("p_ready")
        t_ready = sem("t_ready")
        pt_ready = sem("pt_ready")
        pv_done = sem("pv_done")
        pair_final = sem("pair_final")
        th_ready = sem("th_ready")
        th_used = sem("th_used")
        hn_ready = sem("hn_ready")
        shi_ready = sem("shi_ready")
        slo_ready = sem("slo_ready")
        dve_own = sem("dve_own")
        xg_ready = sem("xg_ready")
        xg7_ready = sem("xg7_ready")
        fin_ready = sem("fin_ready")
        res_act = sem("res_act")
        res_dve = sem("res_dve")

        MISC_COL, MISC_BC = 0, 1
        MISC_V = {0: [2], 1: [3], 2: [4], 3: [6, 8], 4: [10, 11]}
        MISC_MEAN, MISC_LCOL, MISC_LBC = 5, 7, 9
        MISC_L = 12
        V_AT = {5: (0, 0), 13: (1, 0), 17: (2, 0), 25: (3, 0), 28: (3, 1), 34: (4, 0), 36: (4, 1)}
        ROPES = 2 * DPAIRS
        ADD_L = (KD - 1) + 2 * (CT - 1)
        LN_ADDS = KD - 1 + CT - 1
        SQ_L = KD + CT
        STEPS = CT * (TAPS + 1)
        ACC0 = N_CH + 2

        def chunk_src(l, c):
            if c < N_IN:
                return w_in[l, c], KD
            if c < N_IN + CT:
                return w_pw[l, c - N_IN], CT
            return w_out[l, c - N_IN - CT], KD

        def rows_of(c):
            return CT if N_IN <= c < N_IN + CT else KD

        def follows(l, c):
            l, c = (l, c) if c < N_CH else (l + 1, c - N_CH)
            return (l, c) if l < DEPTH else None

        def gate_at(c):
            return 2 * (c - PRE) + 2

        TH_SEQ = [key for _, _, key in sorted(
            [(LN_SILU + 2 * j, 0, ("ln", j)) for j in range(CT)] +
            [(gate_at(c), 1, t) for c, t in enumerate(IN_TILES) if t[0][1] == "g"])]
        TH_L = len(TH_SEQ)
        Y_OF_GATE = {"ag": 0, "bg": 2, "cg": 5}

        def emptied(l, c):
            return ACC0 + N_CH * l + c + 1

        def x_tile(l, k):
            return emptied(l - 1, N_IN + CT + k)

        def bank_of(c):
            return sc[0] if c == 2 else acc[c % 2]

        def v_tile(g):
            return IN_TILES.index(("bv", g) if g < DPAIRS else ("av", g - DPAIRS))

        def rope_of(c):
            kind, j = IN_TILES[c]
            return 2 * j + (kind == "bk") if kind in ("bq", "bk") else None

        def qk_of(c):
            kind, j = IN_TILES[c]
            return (j + (kind[0] == "a") * DPAIRS, kind[1] == "k") if kind[1] in "qk" else None

        HI_AT = {2 * (IN_TILES.index(t) - PRE) + (4 if t[0][0] == "b" else 2): qk_of(IN_TILES.index(t))
                 for t in IN_TILES if t[0][1] in "qk"}

        def tile_at(n):
            return PRE + n // 2, n % 2 == 1

        FINAL = [(sc[0], 0, 0), (sc[1], 1, 0), (tp[0], 2, 0), (tp[1], 3, 0),
                 (ob, 0, 1), (acc[0], 1, 1), (acc[1], 2, 1), (misc, 3, 1)]
        res = pT[:, :, :, :].rearrange("p h k t -> p (h k) t")

        block = ctx.enter_context(nc.Block())

        @block.sync
        def _(sp):
            def load(l, c, wait):
                src, k = chunk_src(l, c)
                if wait:
                    sp.wait_ge(lo_ready, N_CH * l + c - RAW + 1)
                sp.dma_start(raw[:, c % RAW, 0:k, :], src).then_inc(raw_in[c % RAW], 16)

            def load_next(l, c):
                if (f := follows(l, c + LOAD_AHEAD)) is not None:
                    load(*f, True)

            def swap(l, r):
                sp.wait_ge(acc_free, emptied(l, IN_TILES.index(("bk" if r % 2 else "bq", r // 2))))
                for h in range(4):
                    o = 32 * (h ^ 1)
                    sp.dma_start(zsw[32 * h:32 * h + 32, :], zs[o:o + 32, :]).then_inc(swap_in, 16)

            def load_bias(l, un):
                b = un - DUNITS
                sp.wait_ge(m_ready, UNITS * l + (un - 1 if b >= 2 else DUNITS - 4))
                sp.dma_start(bias[:, b % 2, :], nabias[l, b]).then_inc(bias_in[b % 2], 16)

            sp.dma_start(par[:, :], prm[0]).then_inc(par_in, 16)
            load(0, 0, False)
            for i, k in enumerate(K_ORDER):
                sp.dma_start(x[:, k, :], xT[:, k, :]).then_inc(x_in[k], 16)
                if i == X_BEFORE_W1 - 1:
                    load(0, 1, False)
            load(0, RAW, True)
            sp.dma_start(cs[:, :, :], rope).then_inc(const_in, 16)
            sp.dma_start(cnt[:, :], lncnt).then_inc(const_in, 16)
            sp.dma_start(gf[:, :], gfin).then_inc(const_in, 16)
            for c in range(RAW + 1, LOAD_AHEAD):
                load(0, c, True)
            for l in range(DEPTH):
                for c in range(PRE):
                    if (r := rope_of(c)) is not None:
                        swap(l, r)
                    load_next(l, c)
                for n in range(UNITS):
                    c, ends = tile_at(n)
                    if not ends:
                        load_next(l, c)
                    elif (r := rope_of(c)) is not None:
                        swap(l, r)
                    if n == DUNITS - 4:
                        load_bias(l, DUNITS)
                        load_bias(l, DUNITS + 1)
                    if DUNITS <= n < UNITS - 2:
                        load_bias(l, n + 2)
                for c in range(N_IN, N_CH):
                    load_next(l, c)
                    if c == N_IN + CT and l + 1 < DEPTH:
                        sp.wait_ge(ylo_ready, KD * (l + 1))
                        sp.dma_start(par[:, :], prm[l + 1]).then_inc(par_in, 16)
            for i, (_, a, half) in enumerate(FINAL):
                sp.wait_ge((res_act, res_dve)[i % 2], i // 2 + 1)
                sp.dma_start(out[a, :, half * SEQ:(half + 1) * SEQ], res[:, i, :]).then_inc(out_in, 16)
            sp.wait_ge(out_in, 16 * len(FINAL))

        @block.tensor
        def _(pe):
            def products(c, a_hi, a_lo, first=0, end=None, order=None, ready=None, used=None):
                slot, to, K = c % SPL, bank_of(c), rows_of(c)
                end = K if end is None else end
                for i in range(first, end):
                    k = i if order is None else order[i]
                    if ready is not None:
                        pe.wait_ge(ready[0], ready[1] + i + 1)
                    nc.tensor.matmul(to[:, :], w_hi[:, slot, k, :], a_hi[:, k, :], start=i == 0, stop=False)
                    nc.tensor.matmul(to[:, :], w_lo[:, slot, k, :], a_hi[:, k, :], start=False, stop=False)
                    last = nc.tensor.matmul(to[:, :], w_hi[:, slot, k, :], a_lo[:, k, :], start=False, stop=i == K - 1)
                    if i == K - 1:
                        last.then_inc(tile_done, 1)
                    elif used is not None:
                        last.then_inc(used, 1)

            def open_tile(l, c):
                pe.wait_ge(lo_ready, N_CH * l + c + 1)
                if c == 2:
                    if l:
                        pe.wait_ge(m_ready, UNITS * l)
                else:
                    pe.wait_ge(acc_free, emptied(l, c - 2))

            def in_tile(l, c, first=0, end=KD, ready=None):
                if first == 0 and (l, c) != (0, 0):
                    open_tile(l, c)
                products(c, act_hi, act_lo, first, end, order=K_ORDER, ready=ready)

            def take_misc(l, k):
                pe.wait_ge(misc_free, MISC_L * l + k)

            def norm_col(l, k, adds):
                take_misc(l, k)
                pe.wait_ge(add_done, adds)
                for a in range(QT):
                    last = nc.tensor.matmul(misc[:, a * P:(a + 1) * P], ssq[:, a * P:(a + 1) * P], ones[:, :],
                                            start=True, stop=True)
                last.then_inc(misc_ready, 1)

            def norm_bc(l, k, diags):
                take_misc(l, k)
                pe.wait_ge(diag_ready, diags)
                nc.tensor.matmul(misc[:, :], ones[:, :], acc2[:, :], start=True, stop=True).then_inc(misc_ready, 1)

            def scores(l, n):
                g, h, b = unit(n)
                if n % UPP == 0:
                    pe.wait_ge(q_lo, PAIRS * l + g + 1)
                    pe.wait_ge(klo_own, PAIRS * l + g + 1)
                    pe.wait_ge(klo_other, PAIRS * l + g + 1)
                if n >= 2:
                    pe.wait_ge(m_ready, UNITS * l + n - 1)
                q = qs[:, g % 2, h, b * P:(b + 1) * P]
                first, w = (0, SEQ) if g < DPAIRS else (ROWS * NA_LO[b], NKEY)
                for i, k in enumerate((k_hi, k_lo)):
                    last = nc.tensor.matmul(sc[n % 2][:, 0:w], q, k[:, g % 2, h, first:first + w],
                                            start=i == 0, stop=i == 1)
                last.then_inc(s_ready, 1)

            def turn(l, n):
                g, h, b = unit(n)
                pe.wait_ge(p_ready, UNITS * l + n + 1)
                if n >= 2:
                    pe.wait_ge(pt_ready, UNITS * l + n - 1)
                blocks = QT if g < DPAIRS else NKEY // P
                for k in range(blocks):
                    last = nc.tensor.transpose(tp[n % 2][:, k * P:(k + 1) * P],
                                               prob[:, n % PROBS, k * P:(k + 1) * P], ident[:, :])
                last.then_inc(t_ready, 1)

            def turn_v(l, g, rnd):
                pe.wait_ge(acc_free, emptied(l, v_tile(g)))
                take_misc(l, MISC_V[g][rnd])
                for i in range(QT):
                    if g < DPAIRS:
                        src = vT[:, i * P:(i + 1) * P]
                    else:
                        b, half = divmod(rnd * QT + i, 2)
                        first = ROWS * NA_LO[b] + half * P
                        src = vT[:, first:first + P]
                    last = nc.tensor.transpose(misc[:, i * P:(i + 1) * P], src, ident[:, :])
                last.then_inc(misc_ready, 1)

            def values(l, g):
                pe.wait_ge(pt_ready, UNITS * l + UPP * (g + 1))
                pe.wait_ge(misc_free, MISC_L * l + MISC_V[g][-1] + 1)
                if g >= 1:
                    pe.wait_ge(pair_final, PAIRS * l + g)
                if g < DPAIRS:
                    for k in range(QT):
                        for h in range(2):
                            last = nc.tensor.matmul(ob[HD * h:HD * (h + 1), :], v[:, g % 2, k, HD * h:HD * (h + 1)],
                                                    pT[:, h, k, :], start=k == 0, stop=k == QT - 1)
                else:
                    for b in range(QT):
                        for half in range(2):
                            for h in range(2):
                                last = nc.tensor.matmul(ob[HD * h:HD * (h + 1), b * P:(b + 1) * P],
                                                        v[:, g % 2, 2 * b + half, HD * h:HD * (h + 1)],
                                                        pT[:, h, half, b * P:(b + 1) * P],
                                                        start=half == 0, stop=half == 1)
                last.then_inc(pv_done, 1)

            def ln_mean(l):
                take_misc(l, MISC_MEAN)
                pe.wait_ge(add_done, ADD_L * l + LN_ADDS)
                nc.tensor.matmul(misc[:, :], mean_w[:, :], ssq[:, :], start=True, stop=True).then_inc(misc_ready, 1)

            pe.wait_ge(consts, 5)
            for _ in range(WARM):
                nc.tensor.matmul(misc[:, 0:P], ones[:, :], ident[:, :], start=True, stop=True)
            for l in range(DEPTH):
                if l == 0:
                    pe.wait_ge(acc_free, emptied(0, -2))
                    pe.wait_ge(w0_lo, 1)
                    in_tile(0, 0, 0, KD // 2, ready=(xlo_ready, 0))
                    pe.wait_ge(lo_ready, 1)
                    in_tile(0, 0, KD // 2, KD, ready=(xlo_ready, 0))
                else:
                    in_tile(l, 0, ready=(xlo_ready, KD * l))
                for half in range(2, 2 * PRE):
                    in_tile(l, half // 2, half % 2 * KD // 2, (half % 2 + 1) * KD // 2)
                    if half == COL_HALF:
                        norm_col(l, MISC_COL, ADD_L * l + KD - 1)
                    if half == BC_HALF:
                        norm_bc(l, MISC_BC, 2 * l + 1)
                for n in range(SLOTS):
                    if n < UNITS:
                        scores(l, n)
                        in_tile(l, tile_at(n)[0], n % 2 * KD // 2, (n % 2 + 1) * KD // 2)
                    else:
                        c = N_IN + n - UNITS
                        open_tile(l, c)
                        pe.wait_ge(slo_ready, CT * (l + 1))
                        products(c, s_hi, s_lo)
                    if n >= UPP + LAG and n % UPP == LAG and n < UNITS + LAG:
                        values(l, n // UPP - 1)
                    if LAG <= n < UNITS + LAG:
                        turn(l, n - LAG)
                    if n == LN_MEAN:
                        ln_mean(l)
                    if n == LN_COL:
                        norm_col(l, MISC_LCOL, ADD_L * (l + 1))
                    if n == LN_BC:
                        norm_bc(l, MISC_LBC, 2 * l + 2)
                    if n in V_AT:
                        turn_v(l, *V_AT[n])
                values(l, PAIRS - 1)
                c = N_IN + CT
                open_tile(l, c)
                products(c, act_hi, act_lo, order=K_ORDER, ready=(ylo_ready, KD * l))
                for c in range(N_IN + CT + 1, N_CH):
                    open_tile(l, c)
                    products(c, act_hi, act_lo, order=K_ORDER, used=act_used if c == N_CH - 1 else None)
            for i, (to, a, half) in enumerate(FINAL):
                if half == 0:
                    pe.wait_ge(xg_ready, KD // 2)
                else:
                    pe.wait_ge(xg_ready, KD - 1)
                    pe.wait_ge(xg7_ready, 1)
                if i == KD // 2 + 1:
                    norm_col(DEPTH, MISC_COL, ADD_L * DEPTH + KD - 1)
                if to is misc:
                    take_misc(DEPTH, MISC_COL + 1)
                for k in range(KD // 2):
                    last = nc.tensor.transpose(to[:, k * P:(k + 1) * P],
                                               y[:, half * KD // 2 + k, a * P:(a + 1) * P], ident[:, :])
                last.then_inc(fin_ready, 1)

        @block.scalar
        def _(act):
            def split_hi(l, c):
                K = rows_of(c)
                if N_CH * l + c >= SPL:
                    act.wait_ge(tile_done, N_CH * l + c - SPL + 1)
                act.wait_ge(raw_in[c % RAW], 16 * (N_CH // RAW * l + c // RAW + 1))
                nc.scalar.activation(w_hi[:, c % SPL, 0:K, :], raw[:, c % RAW, 0:K, :], ACT.Copy).then_inc(hi_ready, 1)

            def split_next(l, c):
                if (f := follows(l, c + AHEAD)) is not None:
                    split_hi(*f)

            def x_there(l, k):
                if l == 0:
                    act.wait_ge(x_in[k], 16)
                else:
                    act.wait_ge(acc_free, x_tile(l, k))

            def squares(l, i, k):
                x_there(l, k)
                if i >= 2:
                    act.wait_ge(add_done, ADD_L * l + max(1, i - 2))
                nc.scalar.activation(sq[:, i % 2, :], x[:, k, :], ACT.Square)\
                    .then_inc(sq_ready, 1 + POOL_SQ if (l, i) == (0, POOL_SQ) else 1)

            def ln_squares(l, j):
                act.wait_ge(misc_free, MISC_L * l + MISC_MEAN + 1)
                if j >= 2:
                    act.wait_ge(add_done, ADD_L * l + LN_ADDS + 1)
                nc.scalar.activation(sq[:, j % 2, :], y[:, KD - CT + j, :], ACT.Square).then_inc(sq_ready, 1)

            def x_hi(l, i):
                k = K_ORDER[i]
                x_there(l, k)
                if l:
                    if i < KD - 1:
                        act.wait_ge(act_used, (KD - 1) * (l - 1) + i + 1)
                    else:
                        act.wait_ge(tile_done, N_CH * l)
                nc.scalar.activation(act_hi[:, k, :], x[:, k, :], ACT.Copy,
                                     scale=par[:, P_G + k:P_G + k + 1]).then_inc(xhi_ready, 1)

            def tanh(l, key, src):
                i = TH_SEQ.index(key)
                act.wait_ge(th_used, TH_L * l + i)
                nc.scalar.activation(th[:, :], src, ACT.Tanh).then_inc(th_ready, 1)

            def exps(l, n):
                w = SEQ if n < DUNITS else NKEY
                act.wait_ge(m_ready, UNITS * l + n + 1)
                nc.scalar.activation(prob[:, n % PROBS, 0:w], prob[:, n % PROBS, 0:w], ACT.Exp, scale=-1.0,
                                     bias=nmx[:, n % 4:n % 4 + 1],
                                     accum_out=den[:, n % 4:n % 4 + 1]).then_inc(e_ready, 1)

            def qk_split(l, g, is_k):
                if g < DPAIRS:
                    act.wait_ge(zc_ready, ROPES * l + 2 * g + is_k + 1)
                else:
                    act.wait_ge(acc_free, emptied(l, IN_TILES.index(("ak" if is_k else "aq", g - DPAIRS))))
                for h in range(2):
                    own = slice(HD * h, HD * (h + 1))
                    for o in (own, slice(HD * (1 - h), HD * (2 - h)))[:1 + is_k]:
                        last = nc.scalar.activation((k_hi if is_k else qs)[o, g % 2, h, :], zc[own, :], ACT.Copy)
                last.then_inc(qk_hi, 1)

            def empty_turn(l, n):
                g, h, b = unit(n)
                act.wait_ge(t_ready, UNITS * l + n + 1)
                if n % UPP == 0 and g:
                    act.wait_ge(pv_done, PAIRS * l + g)
                kk = QT if g < DPAIRS else NKEY // P
                nc.scalar.activation(pT[:, h, 0:kk, b * P:(b + 1) * P],
                                     tp[n % 2][:, 0:kk * P].rearrange("p (k t) -> p k t", t=P),
                                     ACT.Copy).then_inc(pt_ready, 1)

            def y_hi(l, i):
                k = K_ORDER[i]
                if i == 0:
                    act.wait_ge(tile_done, N_CH * l + N_IN)
                if k >= KD - CT:
                    act.wait_ge(acc_free, emptied(l, N_IN + k - (KD - CT)))
                else:
                    act.wait_ge(pair_final, PAIRS * l + Y_OF_PAIR.index(k) + 1)
                nc.scalar.activation(act_hi[:, k, :], y[:, k, :], ACT.Copy).then_inc(yhi_ready, 1)

            def v_out(l, g, rnd):
                if g >= 2:
                    act.wait_ge(pv_done, PAIRS * l + g - 1)
                act.wait_ge(misc_ready, MISC_L * l + MISC_V[g][rnd] + 1)
                nc.scalar.activation(v[:, g % 2, rnd * QT:(rnd + 1) * QT, :],
                                     misc[:, :].rearrange("p (k t) -> p k t", t=P), ACT.Copy).then_inc(misc_free, 1)

            def with_final_gain(k):
                if k == 0:
                    act.wait_ge(ylo_ready, KD * DEPTH)
                    act.wait_ge(const_in, 48)
                nc.scalar.activation(y[:, k, :], x[:, k, :], ACT.Copy, scale=gf[:, k:k + 1]).then_inc(xg_ready, 1)

            act.wait_ge(raw_in[0], 16)
            nc.scalar.activation(w_hi[:, 0, 0:W0_FIRST, :], raw[:, 0, 0:W0_FIRST, :], ACT.Copy).then_inc(w0_hi, 1)
            for l in range(DEPTH):
                act.wait_ge(par_in, 16 * (l + 1))
                for i in range(KD - 1):
                    x_hi(l, i)
                    if l == 0 and i == 0:
                        nc.scalar.activation(w_hi[:, 0, W0_FIRST:, :], raw[:, 0, W0_FIRST:, :], ACT.Copy)\
                            .then_inc(hi_ready, 1)
                    if l == 0 and i == X_BEFORE_W1 - 1:
                        split_hi(0, 1)
                if l == 0:
                    x_hi(l, KD - 1)
                    for i in range(POOL_SQ, KD):
                        squares(0, i, K_ORDER[i])
                        if i == KD // 2:
                            split_hi(0, 2)
                else:
                    squares(l, KD - 1, KD - 1)
                    x_hi(l, KD - 1)
                for c in range(PRE):
                    split_next(l, c)
                    kind, j = IN_TILES[c]
                    if kind == "cb":
                        mid = u[:, j, HALO:HALO + SEQ]
                        act.wait_ge(acc_free, emptied(l, c))
                        nc.scalar.activation(mid, mid, ACT.Tanh).then_inc(cbt_ready, 1)
                    if (gk := HI_AT.get(2 * (c - PRE) + 2)) is not None:
                        qk_split(l, *gk)
                for n in range(SLOTS):
                    if n > LAG:
                        empty_turn(l, n - LAG - 1)
                    if n < UNITS:
                        exps(l, n)
                        if n % 2 == 0:
                            split_next(l, tile_at(n)[0])
                    else:
                        split_next(l, N_IN + n - UNITS)
                    if n and n in HI_AT:
                        qk_split(l, *HI_AT[n])
                    if n - 1 in V_AT:
                        v_out(l, *V_AT[n - 1])
                    if n == LN_MEAN + 1:
                        for j in range(CT):
                            ln_squares(l, j)
                    j, phase = divmod(n - LN_SILU, 2)
                    if phase == 0 and 0 < j <= CT:
                        j -= 1
                        act.wait_ge(th_used, TH_L * l + TH_SEQ.index(("ln", j)) + 1)
                        nc.scalar.activation(s_hi[:, j, :], y[:, KD - CT + j, :], ACT.Copy).then_inc(shi_ready, 1)
                    j, phase = divmod(n - LN_SILU, 2)
                    if phase == 0 and 0 <= j < CT:
                        act.wait_ge(hn_ready, CT * (l + 1))
                        tanh(l, ("ln", j), y[:, KD - CT + j, :])
                    if n and n % 2 == 0 and n <= UNITS:
                        c = tile_at(n - 1)[0]
                        kind, j = IN_TILES[c]
                        if kind in Y_OF_GATE:
                            act.wait_ge(acc_free, emptied(l, c))
                            tanh(l, (kind, j), y[:, Y_OF_GATE[kind] + j, :])
                    if n >= UNITS:
                        y_hi(l, n - UNITS)
                for i in range(SLOTS - UNITS, KD):
                    y_hi(l, i)
                for c in range(N_IN + CT, N_CH):
                    split_next(l, c)
                    if c > N_IN + CT:
                        k = c - (N_IN + CT) - 1
                        squares(l + 1, k, k)
                        if l == DEPTH - 1:
                            with_final_gain(k)
            squares(DEPTH, KD - 1, KD - 1)
            act.wait_ge(pow_ready, 2 * DEPTH + 1)
            for i in range(0, len(FINAL), 2):
                to, a, _ = FINAL[i]
                act.wait_ge(fin_ready, i + 1)
                nc.scalar.activation(res[:, i, :], to[:, :], ACT.Copy, scale=rcol[:, a:a + 1]).then_inc(res_act, 1)

        @block.gpsimd
        def _(pool):
            def split_lo(l, c):
                K = rows_of(c)
                pool.wait_ge(hi_ready, N_CH * l + c + 1)
                nc.gpsimd.tensor_tensor(w_lo[:, c % SPL, 0:K, :], raw[:, c % RAW, 0:K, :],
                                        w_hi[:, c % SPL, 0:K, :], ALU.subtract).then_inc(lo_ready, 1)

            def split_next(l, c):
                if (f := follows(l, c + AHEAD)) is not None:
                    split_lo(*f)

            def add_squares(l, k, base=0):
                sqs, adds = (SQ_L * l, ADD_L * l) if base == 0 else (SQ_L * l + KD, ADD_L * l + LN_ADDS)
                pool.wait_ge(sq_ready, sqs + k + 1)
                if k >= 2:
                    pool.wait_ge(add_done, adds + k - 1)
                a = sq[:, 0, :] if k == 1 else ssq[:, :]
                nc.gpsimd.tensor_tensor(ssq[:, :], a, sq[:, k % 2, :], ALU.add).then_inc(add_done, 1)

            def root(l, k):
                pool.wait_ge(misc_free, MISC_L * l + k + 1)
                nc.gpsimd.tensor_tensor(rcol[:, :], col[:, :], nhalf[:, :], ALU.pow).then_inc(pow_ready, 1)

            def norm(l, n):
                w = SEQ if n < DUNITS else NKEY
                pool.wait_ge(r_ready, UNITS * l + n + 1)
                nc.gpsimd.tensor_scalar(prob[:, n % PROBS, 0:w], prob[:, n % PROBS, 0:w], rden[:, n % 4:n % 4 + 1],
                                        1.0, ALU.mult, ALU.mult).then_inc(p_ready, 1)

            def rotate(l, r):
                pool.wait_ge(swap_in, 64 * (ROPES * l + r + 1))
                nc.gpsimd.tensor_tensor(zsw, zsw, cs[:, 1, :], ALU.mult).then_inc(t2_ready, 1)

            def k_split_lo(l, g):
                pool.wait_ge(qk_hi, 2 * (PAIRS * l + g + 1))
                nc.gpsimd.tensor_tensor(k_lo[0:HD, g % 2, 0, :], zc[0:HD, :], k_hi[0:HD, g % 2, 0, :],
                                        ALU.subtract).then_inc(klo_own, 1)

            nc.gpsimd.memset(ident[:, :], 0.0).then_inc(consts, 1)
            nc.gpsimd.memset(ones[:, :], 1.0).then_inc(consts, 1)
            nc.gpsimd.memset(mean_w[:, :], 1.0 / CONV_CH).then_inc(consts, 1)
            nc.gpsimd.memset(nhalf[:, :], -0.5).then_inc(consts, 1)
            pool.wait_ge(consts, 4)
            nc.gpsimd.affine_select(out=ident[:, :], in_=ident[:, :], compare_op=ALU.not_equal, fill=1.0, base=0,
                                    pattern=[[-1, P]], channel_multiplier=1).then_inc(consts, 1)
            for i in range(POOL_SQ):
                k = K_ORDER[i]
                pool.wait_ge(x_in[k], 16)
                to = sq[:, i % 2, :] if i else ssq[:, :]
                nc.gpsimd.tensor_tensor(to, x[:, k, :], x[:, k, :], ALU.mult).then_inc(pool_sq, 1)
                if i:
                    pool.wait_ge(pool_sq, i + 1)
                    if i > 1:
                        pool.wait_ge(add_done, i - 1)
                    nc.gpsimd.tensor_tensor(ssq[:, :], ssq[:, :], to, ALU.add).then_inc(add_done, 1)
            pool.wait_ge(lo_ready, 2)
            for l in range(DEPTH):
                if l == 0:
                    split_lo(0, 2)
                    pool.wait_ge(const_in, 48)
                else:
                    add_squares(l, KD - 1)
                root(l, MISC_COL)
                for c in range(PRE):
                    split_next(l, c)
                    if c < PRE - 1 and (r := rope_of(c)) is not None:
                        rotate(l, r)
                    if (gk := HI_AT.get(2 * (c - PRE) + 2)) is not None and gk[1]:
                        k_split_lo(l, gk[0])
                for n in range(UNITS + 1):
                    if n:
                        norm(l, n - 1)
                    if n < UNITS and n % 2 == 0:
                        split_next(l, tile_at(n)[0])
                    if n % 2 and (r := rope_of(tile_at(n - 2)[0])) is not None:
                        rotate(l, r)
                    if (gk := HI_AT.get(n - 1)) is not None and gk[1]:
                        k_split_lo(l, gk[0])
                    if n == LN_SUM:
                        pool.wait_ge(conv_step, STEPS * (l + 1))
                        for j in range(1, CT):
                            a = y[:, KD - CT, :] if j == 1 else ssq[:, :]
                            nc.gpsimd.tensor_tensor(ssq[:, :], a, y[:, KD - CT + j, :], ALU.add).then_inc(add_done, 1)
                            pool.wait_ge(add_done, ADD_L * l + KD - 1 + j)
                    if n == LN_MEAN + 1:
                        for j in range(1, CT):
                            add_squares(l, j, base=1)
                    if n == LN_BC - 2:
                        root(l, MISC_LCOL)
                for c in range(N_IN, N_CH):
                    split_next(l, c)
                    if c >= N_IN + CT + 2:
                        add_squares(l + 1, c - (N_IN + CT) - 1)
            root(DEPTH, MISC_COL)

        @block.vector
        def _(dve):
            own = [0]

            def step(ins):
                own[0] += 1
                ins.then_inc(dve_own, 1)
                dve.wait_ge(dve_own, own[0])

            def column(l, k, width):
                dve.wait_ge(misc_ready, MISC_L * l + k + 1)
                sums = misc[:, :].rearrange("p (a t) -> p a t", a=QT)[:, :, 0]
                nc.vector.tensor_scalar(col[:, :], sums, 1.0 / width, EPS, ALU.mult, ALU.add).then_inc(misc_free, 1)

            def diagonals(i):
                dve.wait_ge(pow_ready, i + 1)
                for a in range(QT):
                    last = nc.vector.tensor_scalar(diag[:, a, :], ident[:, :], rcol[:, a:a + 1], None, ALU.mult)
                last.then_inc(diag_ready, 1)

            def take_factor(l):
                dve.wait_ge(misc_ready, MISC_L * l + MISC_BC + 1)
                nc.vector.tensor_copy(rstd[:, :], misc[:, :]).then_inc(misc_free, 1)
                dve.wait_ge(misc_free, MISC_L * l + MISC_BC + 1)

            def scaled(dst, c, factor):
                return nc.vector.scalar_tensor_tensor(out=dst, in0=bank_of(c)[:, :], scalar=factor, in1=rstd[:, :],
                                                      op0=ALU.mult, op1=ALU.mult)

            def scaled_by_column(dst, c, factor):
                def view(a):
                    return a.rearrange("p (r c) -> p r c", c=GRID_W)
                return nc.vector.scalar_tensor_tensor(out=dst.rearrange("p (c r) -> p r c", c=GRID_W),
                                                      in0=view(bank_of(c)[:, :]), scalar=factor, in1=view(rstd[:, :]),
                                                      op0=ALU.mult, op1=ALU.mult)

            def empty_tile(l, c):
                kind, j = IN_TILES[c]
                dve.wait_ge(tile_done, N_CH * l + c + 1)
                if kind == "cb":
                    scaled(u[:, j, HALO:HALO + SEQ], c, 0.5).then_inc(acc_free, 1)
                elif kind == "ca":
                    half = y[:, KD - CT + j, :]
                    scaled(half, c, 0.5).then_inc(acc_free, 1)
                    dve.wait_ge(acc_free, emptied(l, c))
                    dve.wait_ge(cbt_ready, CT * l + j + 1)
                    mid = u[:, j, HALO:HALO + SEQ]
                    nc.vector.scalar_tensor_tensor(out=mid, in0=mid, scalar=1.0, in1=half, op0=ALU.add,
                                                   op1=ALU.mult).then_inc(u_ready, 1)
                elif kind in ("bq", "bk"):
                    scaled(zs, c, HD ** -0.5 if kind == "bq" else 1.0).then_inc(acc_free, 1)
                    dve.wait_ge(acc_free, emptied(l, c))
                    if kind == "bq" and PAIRS * l + j:
                        dve.wait_ge(klo_own, PAIRS * l + j)
                    if kind == "bk":
                        dve.wait_ge(q_lo, PAIRS * l + j + 1)
                    nc.vector.tensor_tensor(zc[:, :], zs, cs[:, 0, :], ALU.mult).then_inc(dve_own, 1)
                    own[0] += 1
                elif kind in ("bv", "av"):
                    g = j if kind == "bv" else DPAIRS + j
                    if g:
                        dve.wait_ge(misc_free, MISC_L * l + MISC_V[g - 1][-1] + 1)
                    (scaled if kind == "bv" else scaled_by_column)(vT[:, :], c, 1.0).then_inc(acc_free, 1)
                elif kind == "aq":
                    def by_block(a):
                        return a.rearrange("p (r b c) -> p r b c", b=QT, r=ROWS)
                    dve.wait_ge(klo_own, PAIRS * l + DPAIRS + j)
                    ins = nc.vector.tensor_tensor(zc[:, :].rearrange("p (b r c) -> p r b c", b=QT, r=ROWS),
                                                  by_block(bank_of(c)[:, :]), by_block(rstd[:, :]), ALU.mult)
                    ins.then_inc(acc_free, 1)
                elif kind == "ak":
                    dve.wait_ge(q_lo, PAIRS * l + DPAIRS + j + 1)
                    scaled_by_column(zc[:, :], c, HD ** -0.5).then_inc(acc_free, 1)
                else:
                    scaled(y[:, Y_OF_GATE[kind] + j, :], c, 0.5).then_inc(acc_free, 1)

            def rotated(l, r):
                dve.wait_ge(t2_ready, ROPES * l + r + 1)
                dve.wait_ge(dve_own, own[0])
                nc.vector.tensor_tensor(zc[:, :], zc[:, :], zsw, ALU.add).then_inc(zc_ready, 1)

            def split_lo(l, g, is_k):
                dve.wait_ge(qk_hi, 2 * (PAIRS * l + g) + is_k + 1)
                lo, hi = (k_lo, k_hi) if is_k else (qs, qs)
                for h, to in ((0, 1), (1, 0), (1, 1))[:2 + is_k]:
                    own, o = HD * h, HD * to
                    last = nc.vector.tensor_tensor(lo[o:o + HD, g % 2, h, :], zc[own:own + HD, :],
                                                   hi[own:own + HD, g % 2, h, :], ALU.subtract)
                last.then_inc(klo_other if is_k else q_lo, 1)

            def conv_taps(l, first, count):
                for i in range(first, min(first + count, STEPS)):
                    j, t = divmod(i, TAPS + 1)
                    dst = (y[:, KD - CT + j, :], acc2[:, :])[t % 2]
                    if t == 0:
                        dve.wait_ge(u_ready, CT * l + j + 1)
                    if STEPS * l + i:
                        dve.wait_ge(conv_step, STEPS * l + (i if t == TAPS or t < 2 else i - 1))
                    src = u[:, j, t % TAPS:t % TAPS + SEQ]
                    w = par[:, P_W + TAPS * j + t % TAPS:P_W + TAPS * j + t % TAPS + 1]
                    if t == 0:
                        ins = nc.vector.tensor_scalar(dst, src, w, par[:, P_B + j:P_B + j + 1], ALU.mult, ALU.add)
                    elif t == 1:
                        ins = nc.vector.tensor_scalar(dst, src, w, None, ALU.mult)
                    elif t < TAPS:
                        ins = nc.vector.scalar_tensor_tensor(out=dst, in0=src, scalar=w, in1=dst, op0=ALU.mult,
                                                             op1=ALU.add)
                    else:
                        a = y[:, KD - CT + j, :]
                        ins = nc.vector.tensor_tensor(a, a, acc2[:, :], ALU.add)
                    ins.then_inc(conv_step, 1)

            def maxima(l, n):
                g, h, b = unit(n)
                dve.wait_ge(s_ready, UNITS * l + n + 1)
                if n >= PROBS:
                    dve.wait_ge(t_ready, UNITS * l + n - PROBS + 1)
                if g < DPAIRS:
                    w, add = SEQ, cnt[:, P * (QT - 1 - b):P * (QT - 1 - b) + SEQ]
                else:
                    w, i = NKEY, n - DUNITS
                    dve.wait_ge(bias_in[i % 2], 16 * (UPP * l + i // 2 + 1))
                    add = bias[:, i % 2, :]
                nc.vector.tensor_tensor_reduce(out=prob[:, n % PROBS, 0:w], in0=sc[n % 2][:, 0:w], in1=add, scale=-1.0,
                                               scalar=3e38, op0=ALU.add, op1=ALU.min,
                                               accum_out=nmx[:, n % 4:n % 4 + 1]).then_inc(m_ready, 1)

            def reciprocal(l, n):
                dve.wait_ge(e_ready, UNITS * l + n + 1)
                nc.vector.reciprocal(rden[:, n % 4:n % 4 + 1], den[:, n % 4:n % 4 + 1]).then_inc(r_ready, 1)

            def silu(l, key, t):
                dve.wait_ge(th_ready, TH_L * l + TH_SEQ.index(key) + 1)
                nc.vector.scalar_tensor_tensor(out=t, in0=th[:, :], scalar=1.0, in1=t, op0=ALU.add,
                                               op1=ALU.mult).then_inc(th_used, 1)

            def gated(l, g):
                dve.wait_ge(pv_done, PAIRS * l + g + 1)
                gate = ("bg", g) if g < DPAIRS else ("ag", g - DPAIRS)
                dve.wait_ge(th_used, TH_L * l + TH_SEQ.index(gate) + 1)
                t = y[:, Y_OF_PAIR[g], :]
                if g < DPAIRS:
                    ins = nc.vector.tensor_tensor(t, ob[:, :], t, ALU.mult)
                else:
                    t = t.rearrange("p (r b c) -> p r b c", b=QT, r=ROWS)
                    o = ob[:, :].rearrange("p (b r c) -> p r b c", b=QT, r=ROWS)
                    ins = nc.vector.tensor_tensor(t, o, t, ALU.mult)
                ins.then_inc(pair_final, 1)

            def pointwise(l, j):
                dve.wait_ge(tile_done, N_CH * l + N_IN + j + 1)
                dve.wait_ge(th_used, TH_L * l + TH_SEQ.index(("cg", j)) + 1)
                t = y[:, KD - CT + j, :]
                nc.vector.scalar_tensor_tensor(out=t, in0=acc[(N_IN + j) % 2][:, :],
                                               scalar=par[:, P_PB + j:P_PB + j + 1], in1=t, op0=ALU.add,
                                               op1=ALU.mult).then_inc(acc_free, 1)

            def y_lo(l, i):
                k = K_ORDER[i]
                dve.wait_ge(yhi_ready, KD * l + i + 1)
                nc.vector.tensor_tensor(act_lo[:, k, :], y[:, k, :], act_hi[:, k, :], ALU.subtract)\
                    .then_inc(ylo_ready, 1)

            def add_product(l, k):
                c = N_IN + CT + k
                dve.wait_ge(tile_done, N_CH * l + c + 1)
                nc.vector.tensor_tensor(x[:, k, :], x[:, k, :], bank_of(c)[:, :], ALU.add).then_inc(acc_free, 1)

            def add_squares(l, i):
                dve.wait_ge(sq_ready, SQ_L * l + i + 1)
                if i >= 2:
                    dve.wait_ge(add_done, ADD_L * l + i - 1)
                nc.vector.tensor_tensor(ssq[:, :], sq[:, 0, :] if i == 1 else ssq[:, :], sq[:, i % 2, :],
                                        ALU.add).then_inc(add_done, 1)

            def weights_lo(c, first, end):
                return nc.vector.tensor_tensor(w_lo[:, c, first:end, :], raw[:, c, first:end, :],
                                               w_hi[:, c, first:end, :], ALU.subtract)

            def x_lo(l, i):
                k = K_ORDER[i]
                dve.wait_ge(xhi_ready, KD * l + i + 1)
                nc.vector.scalar_tensor_tensor(out=act_lo[:, k, :], in0=x[:, k, :],
                                               scalar=par[:, P_G + k:P_G + k + 1], in1=act_hi[:, k, :],
                                               op0=ALU.mult, op1=ALU.subtract).then_inc(xlo_ready, 1)

            nc.vector.memset(u[:, :, :], 0.0).then_inc(cleared, 1)
            dve.wait_ge(cleared, 1)
            nc.vector.memset(nmx[:, :], 0.0).then_inc(acc_free, ACC0)
            for l in range(DEPTH):
                dve.wait_ge(par_in, 16 * (l + 1))
                step(nc.vector.tensor_scalar(parh[:, :], par[:, P_LG:P_LG + 2 * CT], 0.5, None, ALU.mult))
                if l == 0:
                    dve.wait_ge(w0_hi, 1)
                    weights_lo(0, 0, W0_FIRST).then_inc(w0_lo, 1)
                for i in range(KD):
                    if l and i == X_LATE:
                        add_product(l - 1, KD - 1)
                    x_lo(l, i)
                    if l == 0 and i == 1:
                        dve.wait_ge(hi_ready, 1)
                        weights_lo(0, W0_FIRST, KD).then_inc(lo_ready, 1)
                    if l == 0 and i == X_BEFORE_W1:
                        dve.wait_ge(hi_ready, 2)
                        weights_lo(1, 0, KD).then_inc(lo_ready, 1)
                if l == 0:
                    for i in range(POOL_SQ, KD):
                        add_squares(0, i)
                column(l, MISC_COL, D)
                if l == 0:
                    dve.wait_ge(consts, 5)
                    dve.wait_ge(const_in, 48)
                diagonals(2 * l)
                take_factor(l)
                taps = 0
                for c in range(PRE):
                    if (gk := HI_AT.get(2 * (c - PRE))) is not None:
                        split_lo(l, *gk)
                    empty_tile(l, c)
                    first, second = taps_in(c=c) // 2, taps_in(c=c) - taps_in(c=c) // 2
                    conv_taps(l, taps, first)
                    if c and (r := rope_of(c - 1)) is not None:
                        rotated(l, r)
                    conv_taps(l, taps + first, second)
                    taps += first + second
                for n in range(SLOTS):
                    if n < UNITS:
                        maxima(l, n)
                    if 0 < n <= UNITS:
                        reciprocal(l, n - 1)
                    if n > UPP + LAG and n % UPP == LAG + 1 and n < SLOTS - 1:
                        gated(l, n // UPP - 1)
                    j, phase = divmod(n - LN_SILU, 2)
                    if phase == 1 and 0 < j <= CT:
                        dve.wait_ge(shi_ready, CT * l + j)
                        nc.vector.tensor_tensor(s_lo[:, j - 1, :], y[:, KD - CT + j - 1, :], s_hi[:, j - 1, :],
                                                ALU.subtract).then_inc(slo_ready, 1)
                    if phase == 1 and 0 <= j < CT:
                        silu(l, ("ln", j), y[:, KD - CT + j, :])
                    if n and n % 2 == 1:
                        c = tile_at(n - 2)[0] if 2 <= n <= UNITS + 1 else 0
                        if n >= 2 and IN_TILES[c][0] in Y_OF_GATE:
                            kind, j = IN_TILES[c]
                            silu(l, (kind, j), y[:, Y_OF_GATE[kind] + j, :])
                    if n and n % 2 == 0 and n <= UNITS:
                        if (r := rope_of(tile_at(n - 4)[0])) is not None:
                            rotated(l, r)
                        empty_tile(l, tile_at(n - 1)[0])
                    if (gk := HI_AT.get(n - 1)) is not None:
                        split_lo(l, *gk)
                    conv_taps(l, taps, taps_in(n=n))
                    taps += taps_in(n=n)
                    if n == LN_MEAN:
                        dve.wait_ge(misc_ready, MISC_L * l + MISC_MEAN + 1)
                        for j in range(CT):
                            t = y[:, KD - CT + j, :]
                            last = nc.vector.tensor_tensor(t, t, misc[:, :], ALU.subtract)
                        last.then_inc(misc_free, 1)
                    if n == LN_COL:
                        column(l, MISC_LCOL, CONV_CH)
                    if n == LN_BC - 1:
                        diagonals(2 * l + 1)
                    if n == LN_BC:
                        dve.wait_ge(misc_ready, MISC_L * l + MISC_LBC + 1)
                        for j in range(CT):
                            t = y[:, KD - CT + j, :]
                            last = nc.vector.tensor_tensor(t, t, misc[:, :], ALU.mult)
                        last.then_inc(misc_free, 1)
                        dve.wait_ge(misc_free, MISC_L * l + MISC_LBC + 1)
                        for j in range(CT):
                            t = y[:, KD - CT + j, :]
                            nc.vector.tensor_scalar(t, t, parh[:, j:j + 1], parh[:, CT + j:CT + j + 1], ALU.mult,
                                                    ALU.add).then_inc(hn_ready, 1)
                    if n > UNITS:
                        pointwise(l, n - UNITS - 1)
                        y_lo(l, n - UNITS - 1)
                pointwise(l, CT - 1)
                gated(l, PAIRS - 1)
                for i in range(CT - 1, KD):
                    y_lo(l, i)
                for k in range(KD - 1):
                    add_product(l, k)
            add_product(DEPTH - 1, KD - 1)
            dve.wait_ge(acc_free, ACC0 + N_CH * DEPTH)
            nc.vector.tensor_scalar(y[:, KD - 1, :], x[:, KD - 1, :], gf[:, KD - 1:KD], None, ALU.mult)\
                .then_inc(xg7_ready, 1)
            add_squares(DEPTH, KD - 1)
            column(DEPTH, MISC_COL, D)
            dve.wait_ge(pow_ready, 2 * DEPTH + 1)
            for i in range(1, len(FINAL), 2):
                to, a, _ = FINAL[i]
                dve.wait_ge(fin_ready, i + 1)
                nc.vector.tensor_scalar(res[:, i, :], to[:, :], rcol[:, a:a + 1], None, ALU.mult).then_inc(res_dve, 1)


def by_partition(a):
    *lead, r, c = a.shape
    a = a.reshape(*lead, r // P, P, c // P, P)
    n = len(lead)
    return a.transpose(*range(n), n + 2, n + 1, n, n + 3)


def dil_table():
    diff = np.arange(NEG_TILE)[None, :] - P * (QT - 1) - np.arange(P)[:, None]
    count = np.zeros(diff.shape, np.int64)
    for w, d in PATTERNS:
        count += (np.abs(diff) <= (w // 2) // d * d) & (diff % d == 0)
    return np.where(count > 0, np.log(np.maximum(count, 1)), NEG).astype(np.float32)


def rope_table():
    half = HD // 2
    ang = np.arange(SEQ)[None, :] * 10000.0 ** (-np.arange(half) * 2.0 / HD)[:, None]
    cos, sin = np.cos(ang), np.sin(ang)
    out = np.stack([np.tile(cos, (4, 1)), np.concatenate([-sin, sin, -sin, sin])], 1)
    return np.ascontiguousarray(out.astype(np.float32))


def na_bias(rpb):
    b, r, c = np.meshgrid(np.arange(QT), np.arange(ROWS), np.arange(GRID_W // QT), indexing="ij")
    col = (GRID_W // QT * b + c).reshape(QT, P)
    row = r.reshape(QT, P)
    j, i = np.meshgrid(np.arange(NAW), np.arange(ROWS), indexing="ij")
    i, j = i.ravel(), j.ravel()
    key_col = np.array(NA_LO)[:, None] + j[None, :]
    first = np.clip(col - WIN_COLS // 2, 0, GRID_W - WIN_COLS)
    inside = (key_col[:, None, :] >= first[:, :, None]) & (key_col[:, None, :] < first[:, :, None] + WIN_COLS)
    at_r = i[None, None, :] - row[:, :, None] + ROWS - 1
    at_c = np.clip(key_col[:, None, :] - col[:, :, None] + WIN_COLS - 1, 0, 2 * WIN_COLS - 2)
    full = np.where(inside, rpb[:, :, at_r, at_c], np.float32(NEG))
    L = rpb.shape[0]
    full = full.reshape(L, NA_HEADS // 2, 2, QT, P, NKEY).transpose(0, 1, 3, 2, 4, 5)
    return np.ascontiguousarray(full.reshape(L, 2 * UPP, P, NKEY))


def kernel(x, norm_g, w_in, na_rpb, conv_w, conv_b, conv_ln_g, conv_ln_b, pw_w, pw_b, w_out, final_g):
    import concourse.bacc as bacc
    from concourse.bass_utils import run_bass_kernel_spmd

    x, norm_g, w_in, na_rpb, conv_w, conv_b, conv_ln_g, conv_ln_b, pw_w, pw_b, w_out, final_g = map(
        np.asarray, (x, norm_g, w_in, na_rpb, conv_w, conv_b, conv_ln_g, conv_ln_b, pw_w, pw_b, w_out, final_g))

    def tiles(a):
        return a.reshape(DEPTH, -1, P).transpose(0, 2, 1)

    order = [PART_AT[kind] // P + j for kind, j in IN_TILES]
    taps = conv_w.transpose(0, 2, 1).reshape(DEPTH, CT, P, TAPS).transpose(0, 2, 1, 3).reshape(DEPTH, P, CT * TAPS)
    arrays = {
        "xT": x[0].T.reshape(KD, P, SEQ).transpose(1, 0, 2),
        "w_in": by_partition(w_in)[:, order],
        "w_pw": by_partition(pw_w),
        "w_out": by_partition(w_out),
        "prm": np.concatenate([tiles(norm_g), taps, tiles(conv_b), tiles(conv_ln_g), tiles(conv_ln_b), tiles(pw_b)], 2),
        "gfin": final_g.reshape(KD, P).T,
        "nabias": na_bias(na_rpb),
        "lncnt": dil_table(),
        "rope": rope_table(),
    }
    arrays = {k: np.ascontiguousarray(a) for k, a in arrays.items()}
    nc = bacc.Bacc("TRN2", target_bir_lowering=False, num_devices=1)
    aps = [nc.dram_tensor(k, a.shape, mybir.dt.from_np(a.dtype), kind="ExternalInput").ap() for k, a in arrays.items()]
    aps.append(nc.dram_tensor("out", (QT, P, D), F32, kind="ExternalOutput").ap())
    build(nc, *aps)
    got = run_bass_kernel_spmd(nc, [arrays], core_ids=[0]).results[0]["out"]
    return got.reshape(1, SEQ, D)
```
